# Optimizing a Trainium2 kernel written in Bass

```python
import jax, jax.numpy as jnp
from jax import lax
import numpy as np
import jax
import jax.numpy as jnp

D_MODEL = 1024
BATCH = 1
SEQ = 256
DEPTH = 2

N_A_LAYERS = DEPTH // 2
N_B_LAYERS = DEPTH - N_A_LAYERS
D_FF = 2816
EPS = 1e-6
NEG = -1e30

M_HEADS = 8
M_DV = D_MODEL // M_HEADS
M_DQK = M_DV // 2
M_CHUNK = 64

N_QH = 16
N_KVH = 4
HEAD_DIM = 64
CMP_BLOCK = 32
CMP_STRIDE = 16
CMP_HIDDEN = 256
SEL_BLOCK = 64
SEL_TOPK = 16
WINDOW = 512
Q_BLOCK = 64
FORCE_SCORE = 1e4


def rmsnorm(x, g):
    xf = x.astype(jnp.float32)
    y = xf * lax.rsqrt(jnp.mean(xf * xf, axis=-1, keepdims=True) + EPS)
    return (y * g.astype(jnp.float32)).astype(x.dtype)

def swiglu(h, w_in, w_out):
    a, b = jnp.split(h @ w_in, 2, axis=-1)
    return (jax.nn.silu(a) * b) @ w_out

def masked_softmax(s, mask):
    s = jnp.where(mask, s.astype(jnp.float32), NEG)
    e = jnp.where(mask, jnp.exp(s - jnp.max(s, axis=-1, keepdims=True)), 0.0)
    z = jnp.sum(e, axis=-1, keepdims=True)
    return e / jnp.where(z > 0, z, 1.0)

def mlstm_mixer(h, w_in, b_if, g_head, w_out):
    B, T, _ = h.shape
    H, L = M_HEADS, M_CHUNK
    NC = T // L
    qk_w, v_w = H * M_DQK, H * M_DV
    proj = h @ w_in
    q, k, v, ig, fg, og = jnp.split(
        proj, [qk_w, 2 * qk_w, 2 * qk_w + v_w, 2 * qk_w + v_w + H, 2 * qk_w + v_w + 2 * H], axis=-1)

    def to_chunks(a, d):
        return a.astype(jnp.float32).reshape(B, NC, L, H, d).transpose(0, 3, 1, 2, 4)

    q = to_chunks(q, M_DQK) * (M_DQK ** -0.5)
    k = to_chunks(k, M_DQK)
    v = to_chunks(v, M_DV)
    bif = b_if.astype(jnp.float32)
    log_i = to_chunks(ig, 1)[..., 0] + bif[0][:, None, None]
    log_f = jax.nn.log_sigmoid(to_chunks(fg, 1)[..., 0] + bif[1][:, None, None])

    b = jnp.cumsum(log_f, axis=-1)
    g_tot = b[..., -1]
    a = g_tot[..., None] - b + log_i
    m_loc = jnp.max(a, axis=-1)
    w_loc = jnp.exp(a - m_loc[..., None])
    C_loc = jnp.einsum('bhcl,bhclk,bhclv->bhckv', w_loc, k, v)
    n_loc = jnp.einsum('bhcl,bhclk->bhck', w_loc, k)

    def step(carry, inp):
        C, n, m = carry
        g, Cl, nl, ml = inp
        m_new = jnp.maximum(g + m, ml)
        s_old = jnp.exp(g + m - m_new)
        s_new = jnp.exp(ml - m_new)
        C_new = s_old[..., None, None] * C + s_new[..., None, None] * Cl
        n_new = s_old[..., None] * n + s_new[..., None] * nl
        return (C_new, n_new, m_new), (C, n, m)

    init = (jnp.zeros((B, H, M_DQK, M_DV), jnp.float32),
            jnp.zeros((B, H, M_DQK), jnp.float32),
            jnp.zeros((B, H), jnp.float32))
    xs = (jnp.moveaxis(g_tot, 2, 0), jnp.moveaxis(C_loc, 2, 0),
          jnp.moveaxis(n_loc, 2, 0), jnp.moveaxis(m_loc, 2, 0))
    _, (C_prev, n_prev, m_prev) = lax.scan(step, init, xs)
    C_prev = jnp.moveaxis(C_prev, 0, 2)
    n_prev = jnp.moveaxis(n_prev, 0, 2)
    m_prev = jnp.moveaxis(m_prev, 0, 2)

    causal = jnp.tril(jnp.ones((L, L), bool))
    D = jnp.where(causal, b[..., :, None] - b[..., None, :] + log_i[..., None, :], -jnp.inf)
    inter = b + m_prev[..., None]
    m_t = jnp.maximum(inter, jnp.max(D, axis=-1))
    W = jnp.exp(D - m_t[..., None]) * jnp.einsum('bhctk,bhcsk->bhcts', q, k)
    s_inter = jnp.exp(inter - m_t)
    num = (s_inter[..., None] * jnp.einsum('bhctk,bhckv->bhctv', q, C_prev)
           + jnp.einsum('bhcts,bhcsv->bhctv', W, v))
    den = s_inter * jnp.einsum('bhctk,bhck->bhct', q, n_prev) + jnp.sum(W, axis=-1)
    h_out = num / jnp.maximum(jnp.abs(den), jnp.exp(-m_t))[..., None]
    h_out = h_out.astype(h.dtype).transpose(0, 2, 3, 1, 4).reshape(B, T, H, M_DV)
    h_out = rmsnorm(h_out, g_head).reshape(B, T, H * M_DV)
    return (h_out * jax.nn.sigmoid(og)) @ w_out

def nsa_shared_kv(s, kv_norm, kv_w, cmp_pe, cmp_w1, cmp_w2, k_norm):
    B, T, _ = s.shape
    n_cmp = (T - CMP_BLOCK) // CMP_STRIDE + 1
    kv = rmsnorm(s, kv_norm) @ kv_w
    kc, vc, ks, vs, kw, vw = [a.reshape(B, T, N_KVH, HEAD_DIM) for a in jnp.split(kv, 6, axis=-1)]
    idx = jnp.arange(n_cmp)[:, None] * CMP_STRIDE + jnp.arange(CMP_BLOCK)[None, :]

    def compress(a, pe, w1, w2):
        blk = a[:, idx] + pe[:, None, :]
        flat = blk.transpose(0, 1, 3, 2, 4).reshape(B, n_cmp, N_KVH, CMP_BLOCK * HEAD_DIM)
        return jax.nn.silu(flat @ w1) @ w2

    k_cmp = rmsnorm(compress(kc, cmp_pe[0], cmp_w1[0], cmp_w2[0]), k_norm[0])
    v_cmp = compress(vc, cmp_pe[1], cmp_w1[1], cmp_w2[1])
    ks = rmsnorm(ks, k_norm[1])
    kw = rmsnorm(kw, k_norm[2])
    return (k_cmp, v_cmp, ks, vs, kw, vw)

def cmp_sel_overlap(n_cmp, n_sel):
    c0 = jnp.arange(n_cmp) * CMP_STRIDE
    s0 = jnp.arange(n_sel) * SEL_BLOCK
    ov = (c0[:, None] < s0[None, :] + SEL_BLOCK) & (c0[:, None] + CMP_BLOCK > s0[None, :])
    return ov.astype(jnp.float32)

def nsa_mixer(h, kv, w_in, q_norm, w_out):
    k_cmp, v_cmp, k_sel, v_sel, k_win, v_win = kv
    B, T, _ = h.shape
    G = N_QH // N_KVH
    n_cmp = k_cmp.shape[1]
    n_sel = T // SEL_BLOCK
    top = min(SEL_TOPK, n_sel)
    proj = h @ w_in
    q = proj[..., :N_QH * HEAD_DIM].reshape(B, T, N_KVH, G, HEAD_DIM)
    q = rmsnorm(q, q_norm) * (HEAD_DIM ** -0.5)
    gates = jax.nn.sigmoid(proj[..., N_QH * HEAD_DIM:].astype(jnp.float32)).reshape(B, T, 3, N_KVH, G)

    overlap = cmp_sel_overlap(n_cmp, n_sel)
    cmp_end = jnp.arange(n_cmp) * CMP_STRIDE + CMP_BLOCK - 1
    sel_id = jnp.arange(n_sel)
    ks_blk = k_sel.reshape(B, n_sel, SEL_BLOCK, N_KVH, HEAD_DIM).transpose(0, 3, 1, 2, 4)
    vs_blk = v_sel.reshape(B, n_sel, SEL_BLOCK, N_KVH, HEAD_DIM).transpose(0, 3, 1, 2, 4)
    kw_pad = jnp.pad(k_win, ((0, 0), (WINDOW, 0), (0, 0), (0, 0)))
    vw_pad = jnp.pad(v_win, ((0, 0), (WINDOW, 0), (0, 0), (0, 0)))
    b_ix = jnp.arange(B)[:, None, None, None]
    h_ix = jnp.arange(N_KVH)[None, None, :, None]
    dt = v_sel.dtype

    def block(qb):
        s0 = qb * Q_BLOCK
        t = s0 + jnp.arange(Q_BLOCK)
        qq = lax.dynamic_slice_in_dim(q, s0, Q_BLOCK, axis=1)
        gb = lax.dynamic_slice_in_dim(gates, s0, Q_BLOCK, axis=1).astype(dt)
        s_c = jnp.einsum('bqhgd,bchd->bqhgc', qq, k_cmp)
        p_c = masked_softmax(s_c, (cmp_end[None, :] <= t[:, None])[None, :, None, None, :])
        o_c = jnp.einsum('bqhgc,bchd->bqhgd', p_c.astype(dt), v_cmp)
        imp = jnp.einsum('bqhgc,cj->bqhj', p_c, overlap)
        valid = (sel_id[None, :] * SEL_BLOCK <= t[:, None])
        cur = (t // SEL_BLOCK)[:, None]
        forced = (sel_id[None, :] == 0) | (sel_id[None, :] == cur) | (sel_id[None, :] == cur - 1)
        score = jnp.where((forced & valid)[None, :, None, :], FORCE_SCORE,
                          jnp.where(valid[None, :, None, :], imp, -1.0))
        val, idx = lax.top_k(score, top)
        k_g = ks_blk[b_ix, h_ix, idx]
        v_g = vs_blk[b_ix, h_ix, idx]
        pos = idx[..., None] * SEL_BLOCK + jnp.arange(SEL_BLOCK)
        m_s = (pos <= t[None, :, None, None, None]) & (val >= 0)[..., None]
        s_s = jnp.einsum('bqhgd,bqhksd->bqhgks', qq, k_g).reshape(B, Q_BLOCK, N_KVH, G, top * SEL_BLOCK)
        p_s = masked_softmax(s_s, m_s.reshape(B, Q_BLOCK, N_KVH, 1, top * SEL_BLOCK))
        o_s = jnp.einsum('bqhgn,bqhnd->bqhgd', p_s.astype(dt),
                         v_g.reshape(B, Q_BLOCK, N_KVH, top * SEL_BLOCK, HEAD_DIM))
        k_w = lax.dynamic_slice_in_dim(kw_pad, s0, WINDOW + Q_BLOCK, axis=1)
        v_w = lax.dynamic_slice_in_dim(vw_pad, s0, WINDOW + Q_BLOCK, axis=1)
        kpos = s0 - WINDOW + jnp.arange(WINDOW + Q_BLOCK)
        m_w = (kpos[None, :] <= t[:, None]) & (kpos[None, :] > t[:, None] - WINDOW) & (kpos[None, :] >= 0)
        s_w = jnp.einsum('bqhgd,bkhd->bqhgk', qq, k_w)
        p_w = masked_softmax(s_w, m_w[None, :, None, None, :])
        o_w = jnp.einsum('bqhgk,bkhd->bqhgd', p_w.astype(dt), v_w)
        return (gb[:, :, 0, :, :, None] * o_c + gb[:, :, 1, :, :, None] * o_s
                + gb[:, :, 2, :, :, None] * o_w)

    o = lax.map(block, jnp.arange(T // Q_BLOCK))
    o = jnp.moveaxis(o, 0, 1).reshape(B, T, N_QH * HEAD_DIM)
    return o @ w_out

def first_inputs(seed: int = 0) -> dict:
    key = jax.random.key(seed)
    k = jax.random.split(key, 20)
    f32 = jnp.float32

    def w(kk, shape, fan_in):
        return jax.random.normal(kk, shape, f32) * fan_in ** -0.5

    def gain(kk, shape):
        return 1.0 + 0.02 * jax.random.normal(kk, shape, f32)

    a_in = 2 * M_HEADS * M_DQK + M_HEADS * M_DV + 2 * M_HEADS + D_MODEL
    b_in = N_QH * HEAD_DIM + 3 * N_QH
    nb = jax.random.normal(k[6], (N_A_LAYERS, 2, M_HEADS), f32)
    return {
        "x": jax.random.normal(k[0], (BATCH, SEQ, D_MODEL), f32),
        "ffn_norm": gain(k[1], (DEPTH, 2, D_MODEL)),
        "ffn_w_in": w(k[2], (DEPTH, 2, D_MODEL, 2 * D_FF), D_MODEL),
        "ffn_w_out": w(k[3], (DEPTH, 2, D_FF, D_MODEL), D_FF),
        "mix_norm": gain(k[4], (DEPTH, D_MODEL)),
        "a_w_in": w(k[5], (N_A_LAYERS, D_MODEL, a_in), D_MODEL),
        "a_b_if": jnp.stack([-1.0 + 0.1 * nb[:, 0], 3.0 + 0.5 * nb[:, 1]], axis=1),
        "a_g_head": gain(k[7], (N_A_LAYERS, M_HEADS, M_DV)),
        "a_w_out": w(k[8], (N_A_LAYERS, M_HEADS * M_DV, D_MODEL), M_HEADS * M_DV),
        "kv_norm": gain(k[9], (D_MODEL,)),
        "kv_w": w(k[10], (D_MODEL, 6 * N_KVH * HEAD_DIM), D_MODEL),
        "cmp_pe": 0.02 * jax.random.normal(k[11], (2, CMP_BLOCK, HEAD_DIM), f32),
        "cmp_w1": w(k[12], (2, CMP_BLOCK * HEAD_DIM, CMP_HIDDEN), CMP_BLOCK * HEAD_DIM),
        "cmp_w2": w(k[13], (2, CMP_HIDDEN, HEAD_DIM), CMP_HIDDEN),
        "k_norm": gain(k[14], (3, HEAD_DIM)),
        "b_w_in": w(k[15], (N_B_LAYERS, D_MODEL, b_in), D_MODEL),
        "b_q_norm": gain(k[16], (N_B_LAYERS, HEAD_DIM)),
        "b_w_out": w(k[17], (N_B_LAYERS, N_QH * HEAD_DIM, D_MODEL), N_QH * HEAD_DIM),
    }

def first_block(x, ffn_norm, ffn_w_in, ffn_w_out, mix_norm, a_w_in, a_b_if, a_g_head, a_w_out,
              kv_norm, kv_w, cmp_pe, cmp_w1, cmp_w2, k_norm, b_w_in, b_q_norm, b_w_out):
    h = x
    kv = None
    for layer in range(DEPTH):
        h = h + 0.5 * swiglu(rmsnorm(h, ffn_norm[layer, 0]), ffn_w_in[layer, 0], ffn_w_out[layer, 0])
        hn = rmsnorm(h, mix_norm[layer])
        if layer < N_A_LAYERS:
            h = h + mlstm_mixer(hn, a_w_in[layer], a_b_if[layer], a_g_head[layer], a_w_out[layer])
        else:
            j = layer - N_A_LAYERS
            h = h + nsa_mixer(hn, kv, b_w_in[j], b_q_norm[j], b_w_out[j])
        h = h + 0.5 * swiglu(rmsnorm(h, ffn_norm[layer, 1]), ffn_w_in[layer, 1], ffn_w_out[layer, 1])
        if layer == N_A_LAYERS - 1:
            kv = nsa_shared_kv(h, kv_norm, kv_w, cmp_pe, cmp_w1, cmp_w2, k_norm)
    return h


N_MIXERS = 4
BLOCK_Q = 128
LN_EPS = 1e-5
RMS_EPS = 1e-6
DN_ALPHA = (2 * DEPTH) ** 0.25
DN_BETA = (8 * DEPTH) ** -0.25
ROPE_THETA = 500000.0
ROPE_FRACTION = 4

FOX_HEADS = 8
FOX_HEAD_DIM = D_MODEL // FOX_HEADS

DSA_HEADS = 8
DSA_HEAD_DIM = D_MODEL // DSA_HEADS
DSA_ROPE_DIM = DSA_HEAD_DIM // ROPE_FRACTION
DSA_NOPE_DIM = DSA_HEAD_DIM - DSA_ROPE_DIM
DSA_KV_RANK = 128
IDX_HEADS = 8
IDX_DIM = 64
IDX_ROPE_DIM = IDX_DIM // ROPE_FRACTION
TOPK_MAX = 256

RWKV_HEAD_DIM = 64
RWKV_HEADS = D_MODEL // RWKV_HEAD_DIM
RWKV_DECAY_LORA = 64
RWKV_AAA_LORA = 64
RWKV_GN_EPS = 64e-5

RET_HEADS = 4
RET_HEAD_DIM = D_MODEL // RET_HEADS
RET_CHUNK = 128
RET_THETA = 10000.0


def _layer_norm(x, g, b, eps):
    xf = x.astype(jnp.float32)
    xc = xf - jnp.mean(xf, -1, keepdims=True)
    var = jnp.mean(xc * xc, -1, keepdims=True)
    return (xc * lax.rsqrt(var + eps) * g.astype(jnp.float32) + b.astype(jnp.float32)).astype(x.dtype)

def _rms_norm(x, g, eps):
    xf = x.astype(jnp.float32)
    return (xf * lax.rsqrt(jnp.mean(xf * xf, -1, keepdims=True) + eps) * g.astype(jnp.float32)).astype(x.dtype)

def _split(a, widths):
    idx = [int(v) for v in np.cumsum(widths)[:-1]]
    return jnp.split(a, idx, axis=-1)

def _rope_tables(seq_len, rot_dim, theta):
    inv = 1.0 / (theta ** (jnp.arange(0, rot_dim, 2, dtype=jnp.float32) / rot_dim))
    ang = jnp.arange(seq_len, dtype=jnp.float32)[:, None] * inv[None, :]
    return jnp.cos(ang), jnp.sin(ang)

def _apply_rope(x, cos, sin):
    half = cos.shape[-1]
    bshape = (cos.shape[0],) + (1,) * (x.ndim - 3) + (half,)
    c = cos.reshape(bshape).astype(x.dtype)
    s = sin.reshape(bshape).astype(x.dtype)
    x1, x2, rest = x[..., :half], x[..., half:2 * half], x[..., 2 * half:]
    return jnp.concatenate([x1 * c - x2 * s, x2 * c + x1 * s, rest], axis=-1)

def _to_blocks(a):
    B, S = a.shape[0], a.shape[1]
    a = a.reshape((B, S // BLOCK_Q, BLOCK_Q) + a.shape[2:])
    return jnp.moveaxis(a, 1, 0)

def _from_blocks(a):
    a = jnp.moveaxis(a, 0, 1)
    return a.reshape((a.shape[0], a.shape[1] * a.shape[2]) + a.shape[3:])

def _fox_mixer(x, w_in, b_f, w_out):
    B, S, D = x.shape
    H, dh = FOX_HEADS, FOX_HEAD_DIM
    q, k, v, f_logit, gate = _split(x @ w_in, [H * dh, H * dh, H * dh, H, D])
    q = q.reshape(B, S, H, dh)
    k = k.reshape(B, S, H, dh)
    v = v.reshape(B, S, H, dh)
    log_f = jax.nn.log_sigmoid((f_logit + b_f).astype(jnp.float32))
    cum = jnp.cumsum(log_f, axis=1)
    cum_t = jnp.transpose(cum, (0, 2, 1))
    kpos = jnp.arange(S)
    starts = jnp.arange(S // BLOCK_Q) * BLOCK_Q
    scale = dh ** -0.5

    def block(args):
        q_b, c_b, t0 = args
        s = jnp.einsum('bqhd,bshd->bhqs', q_b, k).astype(jnp.float32) * scale
        s = s + jnp.transpose(c_b, (0, 2, 1))[..., None] - cum_t[:, :, None, :]
        qpos = t0 + jnp.arange(BLOCK_Q)
        s = jnp.where(kpos[None, :] <= qpos[:, None], s, -jnp.inf)
        p = jax.nn.softmax(s, axis=-1).astype(v.dtype)
        return jnp.einsum('bhqs,bshd->bqhd', p, v)

    o = _from_blocks(lax.map(block, (_to_blocks(q), _to_blocks(cum), starts)))
    return (jax.nn.silu(gate) * o.reshape(B, S, D)) @ w_out

def _dsa_mixer(x, cos_a, sin_a, cos_i, sin_i, w_in, kv_norm_g, w_uk, w_uv, w_out):
    B, S, D = x.shape
    H, dh, dr, dc = DSA_HEADS, DSA_HEAD_DIM, DSA_ROPE_DIM, DSA_KV_RANK
    HI, di = IDX_HEADS, IDX_DIM
    q, ckv, kr, qi, ki, wi, gate = _split(x @ w_in, [H * dh, dc, dr, HI * di, di, HI, D])
    q = _apply_rope(q.reshape(B, S, H, dh), cos_a, sin_a)
    q_rope, q_nope = q[..., :dr], q[..., dr:]
    ckv = _rms_norm(ckv, kv_norm_g, RMS_EPS)
    kr = _apply_rope(kr, cos_a, sin_a)
    q_lat = jnp.einsum('bshn,hcn->bshc', q_nope, w_uk)
    q_full = jnp.concatenate([q_lat, q_rope], axis=-1)
    kv_lat = jnp.concatenate([ckv, kr], axis=-1)
    qi = _apply_rope(qi.reshape(B, S, HI, di), cos_i, sin_i)
    ki = _apply_rope(ki, cos_i, sin_i)
    wi = wi.astype(jnp.float32) * HI ** -0.5
    k_sel = min(TOPK_MAX, S // 4)
    kpos = jnp.arange(S)
    starts = jnp.arange(S // BLOCK_Q) * BLOCK_Q

    def block(args):
        qi_b, wi_b, qf_b, t0 = args
        qpos = t0 + jnp.arange(BLOCK_Q)
        isc = jnp.einsum('bqhd,bsd->bqhs', qi_b, ki).astype(jnp.float32) * di ** -0.5
        isc = jnp.einsum('bqhs,bqh->bqs', jax.nn.relu(isc), wi_b)
        isc = jnp.where(kpos[None, None, :] <= qpos[None, :, None], isc, -jnp.inf)
        _, idx = lax.top_k(isc, k_sel)
        valid = idx <= qpos[None, :, None]
        sel = jax.vmap(lambda kv_b, i_b: kv_b[i_b])(kv_lat, idx)
        logits = jnp.einsum('bqhc,bqkc->bhqk', qf_b, sel).astype(jnp.float32) * dh ** -0.5
        logits = jnp.where(valid[:, None], logits, -jnp.inf)
        p = jax.nn.softmax(logits, axis=-1).astype(sel.dtype)
        o_lat = jnp.einsum('bhqk,bqkc->bqhc', p, sel[..., :dc])
        return jnp.einsum('bqhc,hcd->bqhd', o_lat, w_uv)

    o = _from_blocks(lax.map(block, (_to_blocks(qi), _to_blocks(wi), _to_blocks(q_full), starts)))
    return (jax.nn.silu(gate) * o.reshape(B, S, D)) @ w_out

def _rwkv7_mixer(x, mu, w_in, w0, w_lora_a, w_lora_b, a0, a_lora_a, a_lora_b, k_k, k_a, r_k, gn_g, gn_b, w_out):
    B, S, D = x.shape
    H, N = RWKV_HEADS, RWKV_HEAD_DIM
    f32 = jnp.float32
    xx = jnp.pad(x, ((0, 0), (1, 0), (0, 0)))[:, :S] - x
    w_r, w_k, w_v, w_g = jnp.split(w_in, 4, axis=-1)
    r = (x + xx * mu[0]) @ w_r
    xw = x + xx * mu[1]
    k = (x + xx * mu[2]) @ w_k
    v = (x + xx * mu[3]) @ w_v
    xa = x + xx * mu[4]
    g = (x + xx * mu[5]) @ w_g
    w_log = -jax.nn.softplus(-(w0 + jnp.tanh(xw @ w_lora_a) @ w_lora_b)) - 0.5
    decay = jnp.exp(-jnp.exp(w_log.astype(f32)))
    a = jax.nn.sigmoid(a0 + (xa @ a_lora_a) @ a_lora_b)
    kk = (k * k_k).reshape(B, S, H, N).astype(f32)
    kk = kk * lax.rsqrt(jnp.sum(kk * kk, -1, keepdims=True) + 1e-12)
    k = k * (1 + (a - 1) * k_a)
    r = r.reshape(B, S, H, N)
    k = k.reshape(B, S, H, N)
    v = v.reshape(B, S, H, N)
    a = a.reshape(B, S, H, N)
    decay = decay.reshape(B, S, H, N)

    def tm(t):
        return jnp.moveaxis(t.astype(f32), 1, 0)

    def step(state, inp):
        r_t, w_t, k_t, v_t, kk_t, a_t = inp
        sa = jnp.einsum('bhvk,bhk->bhv', state, -kk_t)
        state = (state * w_t[:, :, None, :] + sa[..., None] * (kk_t * a_t)[:, :, None, :]
                 + v_t[..., None] * k_t[:, :, None, :])
        return state, jnp.einsum('bhvk,bhk->bhv', state, r_t)

    state0 = jnp.zeros((B, H, N, N), f32)
    _, ys = lax.scan(step, state0, (tm(r), tm(decay), tm(k), tm(v), tm(kk), tm(a)))
    y = jnp.moveaxis(ys, 0, 1)
    y = _layer_norm(y, gn_g.reshape(H, N), gn_b.reshape(H, N), RWKV_GN_EPS)
    bonus = jnp.sum(r.astype(f32) * k.astype(f32) * r_k, -1, keepdims=True) * v.astype(f32)
    y = (y + bonus).reshape(B, S, D).astype(x.dtype)
    return (jax.nn.silu(g) * y) @ w_out

def _retnet_mixer(x, cos_r, sin_r, w_in, gn_g, w_out):
    B, S, D = x.shape
    H, dk, C = RET_HEADS, RET_HEAD_DIM, RET_CHUNK
    f32 = jnp.float32
    q, k, v, g = jnp.split(x @ w_in, 4, axis=-1)
    q = _apply_rope(q.reshape(B, S, H, dk), cos_r, sin_r)
    k = _apply_rope(k.reshape(B, S, H, dk), cos_r, sin_r) * dk ** -0.5
    v = v.reshape(B, S, H, dk)
    log_g = jnp.log1p(-(2.0 ** (-5.0 - jnp.arange(H, dtype=f32))))
    pos = jnp.arange(C, dtype=f32)
    diff = pos[:, None] - pos[None, :]
    d_mask = jnp.where(diff[None] >= 0, jnp.exp(jnp.maximum(diff, 0.0)[None] * log_g[:, None, None]), 0.0)
    xi = jnp.exp((pos[None, :] + 1.0) * log_g[:, None])
    zeta = jnp.exp((C - 1.0 - pos[None, :]) * log_g[:, None])
    g_c = jnp.exp(C * log_g)
    nc = S // C

    def chunks(t):
        return jnp.transpose(t.reshape(B, nc, C, H, dk), (1, 0, 3, 2, 4)).astype(f32)

    def step(R, inp):
        q_c, k_c, v_c = inp
        inner = jnp.einsum('bhnd,bhmd->bhnm', q_c, k_c) * d_mask[None]
        o = (jnp.einsum('bhnm,bhme->bhne', inner, v_c)
             + jnp.einsum('bhnd,bhde->bhne', q_c, R) * xi[None, :, :, None])
        R = R * g_c[None, :, None, None] + jnp.einsum('bhmd,bhme->bhde', k_c * zeta[None, :, :, None], v_c)
        return R, o

    R0 = jnp.zeros((B, H, dk, dk), f32)
    _, o = lax.scan(step, R0, (chunks(q), chunks(k), chunks(v)))
    o = jnp.transpose(o, (1, 0, 3, 2, 4)).reshape(B, S, H, dk)
    o = _rms_norm(o, gn_g.reshape(H, dk), RMS_EPS).reshape(B, S, D).astype(x.dtype)
    return (jax.nn.silu(g) * o) @ w_out

def second_inputs(seed: int = 0) -> dict:
    key = jax.random.key(seed)
    keys = iter(jax.random.split(key, 40))
    D = D_MODEL
    f32 = jnp.float32

    def nrm(shape, scale):
        return jax.random.normal(next(keys), shape, f32) * scale

    def unif(shape, lo, hi):
        return jax.random.uniform(next(keys), shape, f32, lo, hi)

    w_s = D ** -0.5
    o_s = D ** -0.5 * DN_BETA
    fox_width = 3 * FOX_HEADS * FOX_HEAD_DIM + FOX_HEADS + D
    dsa_width = (DSA_HEADS * DSA_HEAD_DIM + DSA_KV_RANK + DSA_ROPE_DIM
                 + IDX_HEADS * IDX_DIM + IDX_DIM + IDX_HEADS + D)
    return {
        'x': nrm((BATCH, SEQ, D), 1.0),
        'ln_g': 1.0 + nrm((DEPTH, D), 0.02),
        'ln_b': nrm((DEPTH, D), 0.02),
        'fox_w_in': nrm((D, fox_width), w_s),
        'fox_b_f': unif((FOX_HEADS,), 1.0, 5.0),
        'fox_w_out': nrm((D, D), o_s),
        'dsa_w_in': nrm((D, dsa_width), w_s),
        'dsa_kv_norm_g': 1.0 + nrm((DSA_KV_RANK,), 0.02),
        'dsa_w_uk': nrm((DSA_HEADS, DSA_KV_RANK, DSA_NOPE_DIM), DSA_KV_RANK ** -0.5),
        'dsa_w_uv': nrm((DSA_HEADS, DSA_KV_RANK, DSA_HEAD_DIM), DSA_KV_RANK ** -0.5),
        'dsa_w_out': nrm((D, D), o_s),
        'rwkv_mu': unif((6, D), 0.0, 1.0),
        'rwkv_w_in': nrm((D, 4 * D), w_s),
        'rwkv_w0': unif((D,), -6.0, -1.0),
        'rwkv_w_lora_a': nrm((D, RWKV_DECAY_LORA), w_s),
        'rwkv_w_lora_b': nrm((RWKV_DECAY_LORA, D), 0.5 * RWKV_DECAY_LORA ** -0.5),
        'rwkv_a0': nrm((D,), 0.5),
        'rwkv_a_lora_a': nrm((D, RWKV_AAA_LORA), w_s),
        'rwkv_a_lora_b': nrm((RWKV_AAA_LORA, D), 0.5 * RWKV_AAA_LORA ** -0.5),
        'rwkv_k_k': 0.85 + nrm((D,), 0.05),
        'rwkv_k_a': 1.0 + nrm((D,), 0.05),
        'rwkv_r_k': nrm((RWKV_HEADS, RWKV_HEAD_DIM), 0.1),
        'rwkv_gn_g': 1.0 + nrm((D,), 0.02),
        'rwkv_gn_b': nrm((D,), 0.02),
        'rwkv_w_out': nrm((D, D), o_s),
        'ret_w_in': nrm((D, 4 * D), w_s),
        'ret_gn_g': 1.0 + nrm((D,), 0.02),
        'ret_w_out': nrm((D, D), o_s),
    }

def second_block(x, ln_g, ln_b, fox_w_in, fox_b_f, fox_w_out, dsa_w_in, dsa_kv_norm_g, dsa_w_uk, dsa_w_uv,
              dsa_w_out, rwkv_mu, rwkv_w_in, rwkv_w0, rwkv_w_lora_a, rwkv_w_lora_b, rwkv_a0, rwkv_a_lora_a,
              rwkv_a_lora_b, rwkv_k_k, rwkv_k_a, rwkv_r_k, rwkv_gn_g, rwkv_gn_b, rwkv_w_out, ret_w_in,
              ret_gn_g, ret_w_out):
    S = x.shape[1]
    cos_a, sin_a = _rope_tables(S, DSA_ROPE_DIM, ROPE_THETA)
    cos_i, sin_i = _rope_tables(S, IDX_ROPE_DIM, ROPE_THETA)
    cos_r, sin_r = _rope_tables(S, RET_HEAD_DIM, RET_THETA)
    mixers = (
        lambda h: _fox_mixer(h, fox_w_in, fox_b_f, fox_w_out),
        lambda h: _dsa_mixer(h, cos_a, sin_a, cos_i, sin_i, dsa_w_in, dsa_kv_norm_g, dsa_w_uk, dsa_w_uv, dsa_w_out),
        lambda h: _rwkv7_mixer(h, rwkv_mu, rwkv_w_in, rwkv_w0, rwkv_w_lora_a, rwkv_w_lora_b, rwkv_a0,
                               rwkv_a_lora_a, rwkv_a_lora_b, rwkv_k_k, rwkv_k_a, rwkv_r_k, rwkv_gn_g,
                               rwkv_gn_b, rwkv_w_out),
        lambda h: _retnet_mixer(h, cos_r, sin_r, ret_w_in, ret_gn_g, ret_w_out),
    )
    for i in range(DEPTH):
        x = _layer_norm(DN_ALPHA * x + mixers[i % N_MIXERS](x), ln_g[i], ln_b[i], LN_EPS)
    return x


def setup_inputs(seed=0):
    out = dict(first_inputs(seed))
    for name, value in second_inputs(seed + 1).items():
        if name != "x":
            out[name + "_2"] = value
    return out


def reference(
    x, ffn_norm, ffn_w_in, ffn_w_out, mix_norm, a_w_in, a_b_if, a_g_head, a_w_out, kv_norm,
    kv_w, cmp_pe, cmp_w1, cmp_w2, k_norm, b_w_in, b_q_norm, b_w_out, ln_g_2, ln_b_2, fox_w_in_2,
    fox_b_f_2, fox_w_out_2, dsa_w_in_2, dsa_kv_norm_g_2, dsa_w_uk_2, dsa_w_uv_2, dsa_w_out_2,
    rwkv_mu_2, rwkv_w_in_2, rwkv_w0_2, rwkv_w_lora_a_2, rwkv_w_lora_b_2, rwkv_a0_2,
    rwkv_a_lora_a_2, rwkv_a_lora_b_2, rwkv_k_k_2, rwkv_k_a_2, rwkv_r_k_2, rwkv_gn_g_2,
    rwkv_gn_b_2, rwkv_w_out_2, ret_w_in_2, ret_gn_g_2, ret_w_out_2,
):
    x = first_block(
        x, ffn_norm, ffn_w_in, ffn_w_out, mix_norm, a_w_in, a_b_if, a_g_head, a_w_out, kv_norm,
        kv_w, cmp_pe, cmp_w1, cmp_w2, k_norm, b_w_in, b_q_norm, b_w_out,
    )
    return second_block(
        x, ln_g_2, ln_b_2, fox_w_in_2, fox_b_f_2, fox_w_out_2, dsa_w_in_2, dsa_kv_norm_g_2,
        dsa_w_uk_2, dsa_w_uv_2, dsa_w_out_2, rwkv_mu_2, rwkv_w_in_2, rwkv_w0_2, rwkv_w_lora_a_2,
        rwkv_w_lora_b_2, rwkv_a0_2, rwkv_a_lora_a_2, rwkv_a_lora_b_2, rwkv_k_k_2, rwkv_k_a_2,
        rwkv_r_k_2, rwkv_gn_g_2, rwkv_gn_b_2, rwkv_w_out_2, ret_w_in_2, ret_gn_g_2, ret_w_out_2,
    )


_drawn_inputs = setup_inputs


def setup_inputs(seed=0):
    import zlib

    import numpy as np

    out = dict(_drawn_inputs(seed))
    spreads = {}
    factors = {'ffn_norm': 2.954,
     'a_g_head': 5.048,
     'kv_norm': 8.0,
     'cmp_pe': 8.0,
     'k_norm': 8.0,
     'b_q_norm': 8.0,
     'dsa_kv_norm_g_2': 8.0}
    for name, (base, spread) in spreads.items():
        noise = np.random.default_rng([zlib.crc32(name.encode()), seed]).standard_normal(out[name].shape)
        drawn = base * np.exp(spread * noise) if base else spread * noise
        out[name] = jnp.asarray(drawn.astype(out[name].dtype))
    for name, factor in factors.items():
        out[name] = (out[name] * factor).astype(out[name].dtype)
    return out
```

```python
from contextlib import ExitStack

import numpy as np

import concourse.bass as bass
from concourse import mybir

F32 = mybir.dt.float32
F32R = mybir.dt.float32r
U32 = mybir.dt.uint32
I32 = mybir.dt.int32
ALU = mybir.AluOpType
ACT = mybir.ActivationFunctionType
AX = mybir.AxisListType.X

P = 128
D = 1024
T = 256
KT = D // P
NT = T // P
FF = 2816
FC = 256
NI = FF // FC
EPS = 1e-6
LN_EPS = 1e-5
ALPHA = (2 * 2) ** 0.25
BIG = 1e30
PIECE = 2048
RAW = 2
SPL = 6
AHEAD = 4
HEADS = 8
QH, KVH, HD = 16, 4, 64
NCMP = 15

C_ID = 0
C_CAUS = 128
C_CMASK = C_CAUS + 256
C_CKEEP = C_CMASK + 64
C_ROPE_A = C_CKEEP + 64
C_ROPE_I = C_ROPE_A + 64
C_ALL = C_ROPE_I + 32

R_FFN = 0
R_MIX = 32
R_KV = 48
R_HEAD = 56
R_CKV = 64
R_PE = 65
R_QN = 97
R_KN = 98
R_ALL = 101


def rope_table(dim, theta):
    inv = (1.0 / (np.float32(theta) ** (np.arange(0, dim, 2, dtype=np.float32) / np.float32(dim)))).astype(np.float32)
    ang = np.arange(T, dtype=np.float32)[:, None] * inv[None, :]
    both = np.stack([np.cos(ang), np.sin(ang)], 0).astype(np.float32)
    return both.reshape(2, NT, P, dim // 2).transpose(2, 0, 1, 3).reshape(P, -1)


def constant_tables():
    c = np.zeros((P, C_ALL), np.float32)
    i = np.arange(P)
    c[:, C_ID:C_ID + P] = np.eye(P)
    c[:, C_CAUS + P:C_CAUS + 2 * P] = np.where(i[None, :] > i[:, None], BIG, 0)
    t = (np.arange(NT)[None, :, None] * P + i[:, None, None])
    n = np.arange(32)[None, None, :]
    ok = (n < NCMP) & (16 * n + 31 <= t)
    c[:, C_CMASK:C_CMASK + 64] = np.where(ok, 0, BIG).reshape(P, 64)
    c[:, C_CKEEP:C_CKEEP + 64] = ok.reshape(P, 64)
    c[:, C_ROPE_A:C_ROPE_A + 64] = rope_table(32, 500000.0)
    c[:, C_ROPE_I:C_ROPE_I + 32] = rope_table(16, 500000.0)
    return c


def rows(w, k0, k, c0, n):
    return w[k0 * P:(k0 + k) * P, c0:c0 + n].rearrange("(k p) n -> p k n", p=P)


def chunk_pieces(w, c0, n):
    if n * KT <= PIECE:
        return [(rows(w, 0, KT, c0, n), KT * n)]
    return [(rows(w, 4 * a, 4, c0, n), 4 * n) for a in range(2)]


def out_pieces(w):
    return [(rows(w, 2 * a, 2, 0, D), 2 * D) for a in range(4)]


def program(nc, a, out):
    A_CHUNK, B_CHUNK = "A", "B"
    stages = {
        "mlstm": (a["a_w_in"][0], [(A_CHUNK, 2048, 16), (A_CHUNK, 2064, 512), (A_CHUNK, 2576, 512),
                                   (A_CHUNK, 1024, 512), (A_CHUNK, 1536, 512), (B_CHUNK, 0, 512), (B_CHUNK, 512, 512)]),
        "kv": (a["kv_w"], [(A_CHUNK, 0, 512), (A_CHUNK, 512, 512), (A_CHUNK, 1024, 512)]),
        "nsa": (a["b_w_in"][0], [(A_CHUNK, 0, 512), (A_CHUNK, 512, 512), (A_CHUNK, 1024, 48)]),
        "fox": (a["fox_w_in_2"], [(A_CHUNK, 3072, 8), (B_CHUNK, 3080, 512), (B_CHUNK, 3592, 512),
                                  (A_CHUNK, 2048, 512), (A_CHUNK, 2560, 512), (B_CHUNK, 0, 512), (B_CHUNK, 512, 512),
                                  (B_CHUNK, 1024, 512), (B_CHUNK, 1536, 512)]),
        "dsa": (a["dsa_w_in_2"], [(A_CHUNK, 1024, 160), (A_CHUNK, 1696, 72), (A_CHUNK, 1184, 512),
                                  (A_CHUNK, 0, 512), (A_CHUNK, 512, 512), (B_CHUNK, 1768, 512), (B_CHUNK, 2280, 512)]),
    }
    order = ["ffn0", "mlstm", "mlstm_out", "ffn1", "kv", "cmp", "ffn2", "nsa", "nsa_out", "ffn3",
             "fox", "fox_out", "dsa", "dsa_out"]
    outs = {"mlstm_out": a["a_w_out"][0], "nsa_out": a["b_w_out"][0], "fox_out": a["fox_w_out_2"],
            "dsa_out": a["dsa_w_out_2"]}
    first_piece, first_chunk, pieces = {}, {}, []
    n_chunks = 0
    for name in order:
        first_piece[name] = len(pieces)
        first_chunk[name] = n_chunks
        if name.startswith("ffn"):
            pieces += [None] * (3 * NI)
        elif name == "cmp":
            for kv in range(2):
                for half in range(2):
                    pieces.append((rows(a["cmp_w1"][kv], 8 * half, 8, 0, 256), PIECE))
        elif name in outs:
            pieces += out_pieces(outs[name])
        else:
            w, chunks = stages[name]
            for _, c0, n in chunks:
                pieces += chunk_pieces(w, c0, n)
            n_chunks += len(chunks)
    NP = len(pieces)

    with ExitStack() as ctx:
        def sb(name, shape, dt=F32):
            return ctx.enter_context(nc.sbuf_tensor(name, shape, dt))

        def sem(name):
            return ctx.enter_context(nc.semaphore(name))

        PS = ctx.enter_context(nc.psum_tensor("PS", [P, 8, 512], F32))

        raw = sb("raw", [P, RAW, PIECE])
        whi = sb("whi", [P, SPL, PIECE], F32R)
        wlo = sb("wlo", [P, SPL, PIECE], F32R)
        h = sb("h", [P, NT, D])
        XH = sb("XH", [P, KT, T], F32R)
        XL = sb("XL", [P, KT, T], F32R)
        xs = sb("xs", [P, NT, D])
        GH = sb("GH", [P, 2, T], F32R)
        GL = sb("GL", [P, 2, T], F32R)
        scr = sb("scr", [P, 1024])
        con = sb("con", [P, C_ALL])
        par = sb("par", [P, P])
        qgain = sb("qgain", [P, 1])
        w2s = sb("w2s", [P, 2, 2, HD])
        bif = sb("bif", [HEADS, 3])
        ss = sb("ss", [P, 32])
        rv = sb("rv", [P, 32])
        ry = sb("ry", [P, 32])
        rt = sb("rt", [P, 32])
        rr = sb("rr", [P, 32])
        lns = sb("lns", [P, 8])
        nmin = sb("nmin", [P, 96])
        zsum = sb("zsum", [P, 96])
        rz = sb("rz", [P, 96])
        n_cm = sb("n_cm", [P, 3 * 32])
        AW = 12672
        arena = sb("arena", [P, AW])
        rowsb = arena[:, 0:P]

        ffe = scr[:, 0:512].rearrange("p (t c) -> p t c", t=NT)
        ffg = scr[:, 512:1024].rearrange("p (t c) -> p t c", t=NT)
        grow = [scr[0:HEADS, T * r:T * r + T] for r in range(4)]
        ident = con[:, C_ID:C_ID + P]
        caus = con[:, C_CAUS:C_CAUS + 256]
        zcol = con[:, C_CAUS:C_CAUS + 1]
        cmask = con[:, C_CMASK:C_CMASK + 64].rearrange("p (t n) -> p t n", t=NT)
        ckeep = con[:, C_CKEEP:C_CKEEP + 64].rearrange("p (t n) -> p t n", t=NT)

        def carve(start, *sizes):
            views, at = [], start
            for n in sizes:
                views.append(arena[:, at:at + n])
                at += n
            assert at <= AW, (at, AW)
            return views

        m_qT, m_kT, m_v, m_og, m_E, m_g, m_tok = carve(0, 1024, 1024, NT * HEADS * 129, 2048, HEADS * 384, 32, 64)
        m_qT = m_qT.rearrange("p (m t) -> p m t", m=4)
        m_kT = m_kT.rearrange("p (m t) -> p m t", m=4)
        m_v = m_v.rearrange("p (s h d) -> p s h d", s=NT, h=HEADS)
        m_og = m_og.rearrange("p (t d) -> p t d", t=NT)
        m_E = m_E.rearrange("p (h t) -> p h t", h=HEADS)
        m_g = m_g.rearrange("p (t c) -> p t c", t=NT)
        m_a = m_tok[:, 0:16].rearrange("p (t h) -> p t h", t=NT)
        m_floor = m_tok[:, 16:32].rearrange("p (t h) -> p t h", t=NT)
        KTS, VTS, KB, VB, v_k, v_kd, v_cd, v_ct, v_sc, v_scT = carve(
            0, 2 * KVH * T, 2 * NT * T, KVH * 64, 2 * KVH * P, 1024, 2048, 2048, 2048, 256, 256)
        KTS = KTS.rearrange("p (b h t) -> p b h t", b=2, h=KVH)
        VTS = VTS.rearrange("p (b t d) -> p b t d", b=2, t=NT)
        KB = KB.rearrange("p (h n) -> p h n", h=KVH)
        VB = VB.rearrange("p (h k n) -> p h k n", h=KVH, k=2)
        v_k = v_k.rearrange("p (b t h d) -> p b t h d", b=2, t=NT, h=KVH)
        v_kd = v_kd.rearrange("p (b t h u d) -> p b t h u d", b=2, t=NT, h=KVH, u=2)
        v_cd = v_cd.rearrange("p (t c u d) -> p t c u d", t=NT, c=8, u=2)
        v_rep = v_kd.rearrange("p b t h u d -> p (b t h u d)")[:, 0:1024].rearrange(
            "p (k g j n) -> p k g j n", k=2, g=KVH, j=4)
        v_ct = v_ct.rearrange("p (c t) -> p c t", c=8)
        v_scT = v_scT.rearrange("p (k m) -> p k m", k=2)
        v_fs = xs[:, :, :].rearrange("p t d -> p (t d)")[:, 0:960].rearrange("p (l h n) -> p l h n", l=16, h=KVH)
        FH = XH[:, :, :].rearrange("p k t -> p (k t)").rearrange("p (l h n) -> p l h n", l=16, h=KVH)
        FL = XL[:, :, :].rearrange("p k t -> p (k t)").rearrange("p (l h n) -> p l h n", l=16, h=KVH)
        MIX = AW - 4096
        t_S, t_PT = carve(MIX, 2048, 2048)
        wide = t_S
        LNB = t_S.rearrange("p (w d) -> p w d", w=2)
        S_idx = t_S[:, 0:1024].rearrange("p (b n) -> p b n", b=2)
        d_qi = t_S[:, 0:1024].rearrange("p (t c) -> p t c", t=NT)
        d_wukr = t_S[:, 1024:2048].rearrange("p (h n) -> p h n", h=HEADS)
        d_isc, d_work, d_kiT, d_kiwi, d_kid, d_m8, d_w8 = carve(MIX + 2048, 384, 384, 256, 144, 256, 8, 16)
        d_kiwi = d_kiwi.rearrange("p (t c) -> p t c", t=NT)
        d_kid = d_kid.rearrange("p (t u d) -> p t u d", t=NT, u=2)
        d_w8 = d_w8.rearrange("p (t h) -> p t h", t=NT)
        d_ra, d_rb = carve(MIX + 2048 + 1448, 256, 256)
        t_S = t_S.rearrange("p (b j s) -> p b j s", b=2, j=4)
        t_PT = t_PT.rearrange("p (b s j t) -> p b s j t", b=2, s=2, j=4)
        keep = 2 * KVH * T + 2 * NT * T + KVH * 64 + 2 * KVH * P
        n_qT, n_gt, n_cs, n_cpT = carve(keep, 2048, 96, 1024, 1024)
        n_qT = n_qT.rearrange("p (k t) -> p k t", k=KT)
        n_gt = n_gt.rearrange("p (t c) -> p t c", t=NT)
        n_cs = n_cs.rearrange("p (t h n) -> p t h n", t=NT, h=QH)
        n_cpT = n_cpT.rearrange("p (t g q) -> p t g q", t=NT, g=KVH)
        f_qT, f_kT, f_v, f_gate, d_sel = carve(0, 2048, 2048, 2048, 2048, 384)
        f_qT = f_qT.rearrange("p (k t) -> p k t", k=KT)
        f_kT = f_kT.rearrange("p (k t) -> p k t", k=KT)
        f_v = f_v.rearrange("p (s d) -> p s d", s=NT)
        f_gate = f_gate.rearrange("p (k t) -> p k t", k=KT)
        f_cm = xs[:, :, :].rearrange("p t d -> p (t d)").rearrange("p (h s) -> p h s", h=HEADS)
        z_mix = scr[:, :].rearrange("p (k t) -> p k t", k=KT)
        f_f = n_cm[:, 0:16].rearrange("p (t c) -> p t c", t=NT)
        d_qT, d_ql = carve(0, 2048, 2048)
        d_qT = d_qT.rearrange("p (k t) -> p k t", k=KT)
        d_ql = d_ql.rearrange("p (k t) -> p k t", k=KT)
        d_ckr, d_ckvT, d_krT, d_wuv = carve(4096, 320, 256, 256, 1024)
        d_ckr = d_ckr.rearrange("p (t c) -> p t c", t=NT)
        d_wuv = d_wuv.rearrange("p (h d) -> p h d", h=HEADS)
        d_qiT = d_ql[:, 0:4, :]
        d_ol = xs[:, 0, :].rearrange("p (k t) -> p k t", k=KT)
        d_wukT = scr[:, :].rearrange("p (h c) -> p h c", h=HEADS)

        x_in = sem("x_in")
        con_in = sem("con_in")
        params_in = sem("params_in")
        small_in = sem("small_in")
        wuk_in = sem("wuk_in")
        ln_in = sem("ln_in")
        landed = [sem(f"landed{r}") for r in range(RAW)]
        hi_done = sem("hi_done")
        lo_done = sem("lo_done")
        used = sem("used")
        par_ps = sem("par_ps")
        par_ready = sem("par_ready")
        pads_ready = sem("pads_ready")
        ss_act = sem("ss_act")
        root_out = sem("root_out")
        act_step = sem("act_step")
        dve_step = sem("dve_step")
        xs_act = sem("xs_act")
        xs_dve = sem("xs_dve")
        turned = sem("turned")
        turned_hi = sem("turned_hi")
        x_ready = sem("x_ready")
        a_ready = sem("a_ready")
        exp_done = sem("exp_done")
        silu_step = sem("silu_step")
        gated = sem("gated")
        g_turned = sem("g_turned")
        gh_done = sem("gh_done")
        gl_done = sem("gl_done")
        first_tile = sem("first_tile")
        acc_first = sem("acc_first")
        h_first = sem("h_first")
        h_ready = sem("h_ready")
        chunk_ps = sem("chunk_ps")
        chunk_act = sem("chunk_act")
        chunk_dve = sem("chunk_dve")
        side_ps = sem("side_ps")
        side_act = sem("side_act")
        side_dve = sem("side_dve")
        side_src = sem("side_src")
        by_act = sem("by_act")
        m_diag = sem("m_diag")
        head_sq = sem("head_sq")
        m_decay = sem("m_decay")
        m_st = sem("m_st")
        m_w = sem("m_w")
        m_num = sem("m_num")
        m_out = sem("m_out")
        s_ready = sem("s_ready")
        masked = sem("masked")
        expd = sem("expd")
        scaled = sem("scaled")
        pt_ps = sem("pt_ps")
        pt_act = sem("pt_act")
        pt_dve = sem("pt_dve")
        pv_done = sem("pv_done")
        z_raw = sem("z_raw")
        z_hi = sem("z_hi")
        z_ready = sem("z_ready")
        cs_ps = sem("cs_ps")
        cs_neg = sem("cs_neg")
        cs_exp = sem("cs_exp")
        q_norm = sem("q_norm")
        q_ps = sem("q_ps")
        qT_act = sem("qT_act")
        qT_dve = sem("qT_dve")
        for_act = sem("for_act")
        ol_ready = sem("ol_ready")
        uv_done = sem("uv_done")
        idx_acc = sem("idx_acc")
        out_sent = sem("out_sent")

        roots = ["ffn0", "mlstm", "head", "ffn1", "kv", "keys", "kcmp", "ffn2", "nsa", "q", "ffn3", "ln0", "ckv", "ln1"]
        rms = ["ffn0", "mlstm", "ffn1", "kv", "ffn2", "nsa", "ffn3"]
        turns = ["ffn0", "mlstm", "mlstm_out", "ffn1", "kv", "ffn2", "nsa", "ffn3", "fox", "dsa"]
        gains = {"ffn0": R_FFN, "ffn1": R_FFN + 8, "ffn2": R_FFN + 16, "ffn3": R_FFN + 24, "mlstm": R_MIX,
                 "nsa": R_MIX + 8, "kv": R_KV, "mlstm_out": R_HEAD}
        updates = {"ffn0": 1, "mlstm_out": 2, "ffn1": 3, "ffn2": 4, "nsa_out": 5, "ffn3": 6, "ln0": 7, "ln1": 8}
        before = {"ffn0": 0, "mlstm": 1, "ffn1": 2, "kv": 3, "ffn2": 3, "nsa": 4, "ffn3": 5}
        sides = ([("m_rows", "act"), ("m_a", "dve"), ("m_floor", "act")] + [(f"m_M{j}", "act") for j in range(4)]
                 + [("ct0", "act"), ("ct1", "dve"), ("ct2", "act"), ("ct3", "dve")]
                 + [("kt0", "act"), ("kt1", "dve"), ("kt2", "act"), ("kt3", "dve")]
                 + [("c0", "source"), ("c0T", "act"), ("kcmp", "dve"), ("kcmpT", "dve"),
                    ("c1", "source"), ("c1T", "act"), ("vcmp", "dve")]
                 + [("f_rows", "act")] + [(f"f_C{j}", "dve") for j in range(4)]
                 + [("wuk0", "act"), ("wuk1", "dve"), ("qi0", "act"), ("qi1", "dve"), ("ki_ckv", "act"), ("kr", "dve")]
                 + [(f"idx{j}", "act") for j in range(6)]
                 + [("ql0", "act"), ("ql1", "dve"), ("ql2", "act"), ("ql3", "dve")])
        side_no = {name: k for k, (name, _) in enumerate(sides)}
        sources = ["m_a", "m_floor", "keys", "c0", "c0T", "kcmpT", "c1", "c1T", "f_cum", "qi", "ki_ckv"]
        for_act_names = ["abs0", "block0", "block1", "abs1", "ln0", "ln1"]
        for_act_no = {name: k + 1 for k, name in enumerate(for_act_names)}
        by_act_names = ["log0", "og", "fh0", "c0", "fh1", "c1", "gates", "log1", "ln0", "ln1"]
        by_act_no = {name: k + 1 for k, name in enumerate(by_act_names)}
        src_no = {name: k + 1 for k, name in enumerate(sources)}
        unit0 = {"nsa": 0, "fox": 16, "dsa": 20}
        units = {"nsa": [(t, g, b) for t in range(NT) for g in range(KVH) for b in range(2)],
                 "fox": [(t, g, 0) for t in range(NT) for g in range(2)],
                 "dsa": [(t, g, 0) for t in range(NT) for g in range(2)]}
        unit_t = [t for st in ("nsa", "fox", "dsa") for t, _, _ in units[st]]
        zstage = {"nsa": 0, "fox": 1, "dsa": 2}

        def looks(k, who):
            return sum(1 for _, w in sides[:k + 1] if w == who)

        def made(k):
            return sum(1 for name, _ in sides[:k + 1] if name not in ("c0", "c1"))

        def chunk_end(stage, c):
            return first_piece[stage] + sum(2 if n * KT > PIECE else 1 for _, _, n in stages[stage][1][:c + 1])

        def piece_end(stage):
            later = [p for p in first_piece.values() if p > first_piece[stage]]
            return min(later) if later else NP

        def counted(it, by, first):
            return first if it is None else it * by + first

        def place(j, w):
            return 512 * (j % 2) + w * (j // 2)

        index_parts = [(0, (0, 2, 4, 6)), (0, (1, 3, 5, 7)), (1, (0, 2)), (1, (4, 6)), (1, (1, 3)), (1, (5, 7))]

        def second_tiles(u):
            return sum(unit_t[:u + 1])

        O_ps = PS[:, 6:8, :].rearrange("p b (k t) -> p (b k) t", t=P)
        acc_ps = PS[:, 0:4, :].rearrange("p (t w) n -> p t w n", t=NT)

        block = ctx.enter_context(nc.Block())

        @block.sync
        def _(sp):
            sp.dma_start(h[:, 1, :], a["x"][0, P:T, :]).then_inc(x_in, 16)

            def free_raw(p):
                if p >= RAW:
                    sp.wait_ge(lo_done, p - RAW + 1)

            for name in order:
                p0 = first_piece[name]
                if not name.startswith("ffn"):
                    last = NP
                    for o in order:
                        if first_piece[o] > p0:
                            last = min(last, first_piece[o])
                    for p in range(p0, last):
                        free_raw(p)
                        src, n = pieces[p]
                        k = src.shape[1]
                        dst = raw[:, p % RAW, 0:n].rearrange("p (k n) -> p k n", k=k)
                        for part in (slice(0, k // 2), slice(k // 2, k)):
                            sp.dma_start(dst[:, part, :], src[:, part, :]).then_inc(landed[p % RAW], 16)
                    continue
                f = int(name[3])
                w_in, w_out = a["ffn_w_in"][f // 2, f % 2], a["ffn_w_out"][f // 2, f % 2]
                w_in = w_in.rearrange("(k p) (w n) -> p k w n", p=P, w=2)
                w_out = w_out.rearrange("(k p) n -> p k n", p=P)

                def load_in(p, half, i):
                    dst = raw[:, p % RAW, :].rearrange("p (k w n) -> p k w n", k=4, w=2)
                    for w in range(2):
                        sp.dma_start(dst[:, :, w, :], w_in[:, 4 * half:4 * half + 4, w, i])\
                            .then_inc(landed[p % RAW], 16)

                def load_out(p, k2):
                    dst = raw[:, p % RAW, :].rearrange("p (k n) -> p k n", k=2)
                    for w in range(2):
                        cols = slice(512 * w, 512 * w + 512)
                        sp.dma_start(dst[:, :, cols], w_out[:, k2, cols]).then_inc(landed[p % RAW], 16)

                for half in range(2):
                    free_raw(p0 + half)
                    load_in(p0 + half, half, slice(0, FC))
                with nc.sync.Fori(0, (NI - 1) // 2) as it:
                    for i in (1, 2):
                        for j in range(3):
                            p = p0 + 2 + 3 * (i - 1) + j
                            sp.wait_ge(lo_done, it * 6 + (p - RAW + 1))
                            if j < 2:
                                load_in(p, j, bass.ds(it * (2 * FC) + i * FC, FC))
                            else:
                                load_out(p, bass.ds(it * 4 + 2 * (i - 1), 2))
                p = p0 + 3 * NI - 1
                free_raw(p)
                load_out(p, slice(2 * NI - 2, 2 * NI))
            sp.wait_ge(first_tile, 2)
            sp.dma_start(out[0, 0:P, :], h[:, 0, :]).then_inc(out_sent, 16)
            sp.wait_ge(h_ready, updates["ln1"])
            sp.dma_start(out[0, P:T, :], h[:, 1, :]).then_inc(out_sent, 16)
            sp.wait_ge(out_sent, 32)

        @block.gpsimd
        def _(pool):
            pool.memset(rowsb[:, :], 0.0).then_inc(pads_ready, 1)
            pool.wait_ge(pads_ready, 1)

            def load_rows(r, n, src):
                pool.dma_start(rowsb[r:r + n, :], src).then_inc(params_in, 16)

            load_rows(R_FFN, 32, a["ffn_norm"].rearrange("l s (k p) -> (l s k) p", p=P))
            load_rows(R_MIX, 16, a["mix_norm"].rearrange("l (k p) -> (l k) p", p=P))
            load_rows(R_KV, 8, a["kv_norm"].rearrange("(k p) -> k p", p=P))
            load_rows(R_HEAD, 8, a["a_g_head"][0])
            load_rows(R_CKV, 1, a["dsa_kv_norm_g_2"].rearrange("(a p) -> a p", a=1))
            load_rows(R_PE, 32, a["cmp_pe"].rearrange("c (l u) d -> (c l) (u d)", u=2))
            for half in range(2):
                pool.dma_start(rowsb[R_QN:R_QN + 1, 64 * half:64 * half + 64], a["b_q_norm"]).then_inc(params_in, 16)
                pool.dma_start(rowsb[R_KN:R_KN + 3, 64 * half:64 * half + 64], a["k_norm"]).then_inc(params_in, 16)
            pool.dma_start(w2s[:, :, :, :], a["cmp_w2"].rearrange("c (k p) d -> p c k d", p=P)).then_inc(small_in, 16)
            pool.dma_start(bif[:, 0:2], a["a_b_if"][0].rearrange("c h -> h c"), allow_slow_non_contiguous=True).then_inc(small_in, 16)
            pool.dma_start(bif[:, 2:3], a["fox_b_f_2"].rearrange("(h c) -> h c", c=1), allow_slow_non_contiguous=True).then_inc(small_in, 16)
            pool.memset(m_v[:, :, :, 128:129], 1.0).then_inc(pads_ready, 1)
            for j in range(HEADS // 2):
                pool.wait_ge(m_decay, j + 1)
                for blk in (slice(0, P), slice(256, 384)):
                    two_heads = m_E[:, 2 * j:2 * j + 2, blk]
                    pool.affine_select(out=two_heads, in_=two_heads, compare_op=ALU.is_ge, fill=0.0, base=0,
                                       pattern=[[0, 2], [1, P]], channel_multiplier=-1).then_inc(m_diag, 1)
            pool.wait_ge(h_ready, updates["mlstm_out"])
            pool.memset(KB[:, :, :], 0.0).then_inc(pads_ready, 1)
            pool.memset(VB[:, :, :, :], 0.0).then_inc(pads_ready, 1)
            pool.wait_ge(used, first_piece["cmp"])
            pool.memset(FH.bitcast(F32), 0.0).then_inc(pads_ready, 1)
            pool.memset(FL.bitcast(F32), 0.0).then_inc(pads_ready, 1)
            for i, name in enumerate(["fox_out", "dsa_out"]):
                pool.wait_ge(z_ready, 2 * (i + 2))
                pool.dma_start(LNB[:, 0, :], a["ln_g_2"][i:i + 1, :].to_broadcast([P, D])).then_inc(ln_in, 16)
                pool.dma_start(LNB[:, 1, :], a["ln_b_2"][i:i + 1, :].to_broadcast([P, D])).then_inc(ln_in, 16)
                if i == 0:
                    pool.wait_ge(h_ready, updates["ln0"])
                    pool.memset(d_wukr[:, :, 0:32], 0.0).then_inc(pads_ready, 1)
                    pool.dma_start(d_wukr[:, :, 32:128], a["dsa_w_uk_2"].rearrange("h c n -> c h n")).then_inc(wuk_in, 16)
                    pool.dma_start(d_wuv[:, :, :], a["dsa_w_uv_2"].rearrange("h c d -> c h d")).then_inc(wuk_in, 16)

        @block.tensor
        def _(pe):
            mm, tr = nc.tensor.matmul, nc.tensor.transpose

            def three(o, xh, xl, wh, wl, start, stop):
                mm(o, xl, wh, start=start, stop=False, skip_group_check=True)
                mm(o, xh, wl, start=False, stop=False, skip_group_check=True)
                return mm(o, xh, wh, start=False, stop=stop, skip_group_check=True)

            def product(o, terms, start, stop):
                for i, (xh, xl, wh, wl) in enumerate(terms):
                    mm(o, xl, wh, start=start and i == 0, stop=False, skip_group_check=True)
                    mm(o, xh, wl, start=False, stop=False, skip_group_check=True)
                for i, (xh, _, wh, _) in enumerate(reversed(terms)):
                    last = mm(o, xh, wh, start=False, stop=stop and i == len(terms) - 1, skip_group_check=True)
                return last

            def parts(p, k):
                return (whi[:, p % SPL, :].rearrange("p (k n) -> p k n", k=k),
                        wlo[:, p % SPL, :].rearrange("p (k n) -> p k n", k=k))

            late = [0]

            def turn(name):
                u = turns.index(name)
                src = h if name in ("fox", "dsa") else xs
                pe.wait_ge(xs_act, sum(1 for n in turns[:u + 1] if n in rms))
                pe.wait_ge(xs_dve, u + 1)
                for j in range(4):
                    for k in (2 * j, 2 * j + 1):
                        for t in range(NT):
                            last = tr(PS[:, 4 + j, (k % 2) * T + t * P:(k % 2) * T + t * P + P],
                                      src[:, t, k * P:k * P + P], ident)
                    last.then_inc(turned, 1)
                pe.wait_ge(x_ready, 4 * u + 2)
                late[0] = 4 * (u + 1)

            def out_piece(p, k0, XHs, XLs, first, last_piece):
                wh, wl = parts(p, 2)
                for t in range(NT):
                    for w in range(2):
                        last = product(acc_ps[:, t, w, :],
                                       [(XHs[:, k0 + k, t * P:t * P + P], XLs[:, k0 + k, t * P:t * P + P],
                                         wh[:, k, 512 * w:512 * w + 512], wl[:, k, 512 * w:512 * w + 512])
                                        for k in range(2)], start=first, stop=last_piece)
                    if last_piece and t == 0:
                        last.then_inc(acc_first, 1)
                last.then_inc(used, 1)

            def ffn(f):
                p0, n0 = first_piece[f"ffn{f}"], f * NI

                def in_step(p, slot, free):
                    for t in range(NT):
                        if free is not None:
                            pe.wait_ge(gated, free + t)
                        for half in range(2):
                            if t == 0:
                                pe.wait_ge(lo_done, p + (half + 1))
                            if free is None and t == 0 and half == 1:
                                pe.wait_ge(x_ready, late[0])
                            wh, wl = parts(slot + half, 4)
                            for k in range(4):
                                kk = 4 * half + k
                                last = three(PS[:, 4 + t, :], XH[:, kk, t * P:t * P + P], XL[:, kk, t * P:t * P + P],
                                             wh[:, k, :], wl[:, k, :], start=kk == 0, stop=kk == 7)
                            if t == 1:
                                last.then_inc(used, 1)
                        if t == 0:
                            last.then_inc(a_ready, 1)

                def out_step(slot, first, last_step):
                    out_piece(slot, 0, GH, GL, first, last_step)

                def turn_g(gated_n):
                    pe.wait_ge(gated, gated_n)
                    for k in range(2):
                        for t in range(NT):
                            last = tr(PS[:, 6, k * T + t * P:k * T + t * P + P], ffg[:, t, k * P:k * P + P], ident)
                    last.then_inc(g_turned, 1)

                in_step(p0, p0, None)
                turn_g(2 * n0 + 2)
                in_step(p0 + 2, p0 + 2, 2 * n0 + 1)
                pe.wait_ge(gl_done, n0 + 1)
                pe.wait_ge(lo_done, p0 + 5)
                out_step(p0 + 4, True, False)
                turn_g(2 * n0 + 4)
                with nc.tensor.Fori(0, (NI - 3) // 2) as it:
                    for j in range(2):
                        i, p = 2 + j, p0 + 2 + 3 * (1 + j)
                        in_step(it * 6 + p, p, it * 4 + (2 * (n0 + i) - 1))
                        pe.wait_ge(gl_done, it * 2 + (n0 + i))
                        pe.wait_ge(lo_done, it * 6 + (p + 3))
                        out_step(p + 2, False, False)
                        turn_g(it * 4 + (2 * (n0 + i) + 2))
                i, p = NI - 1, p0 + 2 + 3 * (NI - 2)
                in_step(p, p, 2 * (n0 + i) - 1)
                pe.wait_ge(gl_done, n0 + i)
                pe.wait_ge(lo_done, p + 3)
                out_step(p + 2, False, False)
                turn_g(2 * (n0 + i) + 2)
                pe.wait_ge(gl_done, n0 + NI)
                pe.wait_ge(lo_done, p + 4)
                out_step(p + 3, False, True)

            def chunk(stage, c):
                kind, _, n = stages[stage][1][c]
                q = first_chunk[stage] + c
                b0 = 2 * (q % 3)
                end = chunk_end(stage, c)
                if q >= 3:
                    pe.wait_ge(chunk_act, q - 2)
                    pe.wait_ge(chunk_dve, q - 2)
                whole = n * KT <= PIECE
                ps = [(end - 1, 8)] if whole else [(end - 2, 4), (end - 1, 4)]
                pe.wait_ge(lo_done, end)
                tiles = range(NT) if kind == A_CHUNK else range(n // P)
                for m in tiles:
                    for i, (p, kn) in enumerate(ps):
                        if c == 0 and m == 0 and (whole or i == 1):
                            pe.wait_ge(x_ready, late[0])
                        wh, wl = parts_n(p, kn, n)
                        if kind == A_CHUNK:
                            o = PS[:, b0 + m, 0:n]
                            terms = [(XH[:, kn * i + k, m * P:m * P + P], XL[:, kn * i + k, m * P:m * P + P],
                                      wh[:, k, :], wl[:, k, :]) for k in range(kn)]
                        else:
                            o = PS[:, b0 + m // 2, (m % 2) * T:(m % 2) * T + T]
                            cols = slice(m * P, m * P + P)
                            terms = [(wh[:, k, cols], wl[:, k, cols], XH[:, kn * i + k, :], XL[:, kn * i + k, :])
                                     for k in range(kn)]
                        last = product(o, terms, start=i == 0, stop=i == len(ps) - 1)
                        if m == tiles[-1]:
                            last.then_inc(used, 1)
                    if m == tiles[len(tiles) // 2 - 1]:
                        last.then_inc(chunk_ps, 1)

            def parts_n(p, k, n):
                return (whi[:, p % SPL, 0:k * n].rearrange("p (k n) -> p k n", k=k),
                        wlo[:, p % SPL, 0:k * n].rearrange("p (k n) -> p k n", k=k))

            def out_stage(name):
                p0 = first_piece[name]
                for i in range(4):
                    pe.wait_ge(lo_done, p0 + i + 1)
                    if i == 2 and name == "mlstm_out":
                        pe.wait_ge(x_ready, late[0])
                    out_piece(p0 + i, 2 * i, XH, XL, i == 0, i == 3)

            def side(name):
                k = side_no[name]
                if k >= 2 and looks(k - 2, "act"):
                    pe.wait_ge(side_act, looks(k - 2, "act"))
                if k >= 2 and looks(k - 2, "dve"):
                    pe.wait_ge(side_dve, looks(k - 2, "dve"))
                return PS[:, 6 + k % 2, :]

            def attend(stage, scores, values, finish=None):
                todo, u0 = units[stage], unit0[stage]

                def score(i):
                    t, g, b = todo[i]
                    u, w = u0 + i, P * (todo[i][0] + 1)
                    if i >= 2:
                        pe.wait_ge(masked, 4 * (u - 1))
                    bank = PS[:, 2 * (u % 2):2 * (u % 2) + 2, :].rearrange("p b n -> p (b n)")
                    for j in range(4):
                        last = scores(bank[:, place(j, w):place(j, w) + w], t, g, b, j, w)
                    last.then_inc(s_ready, 1)

                def turn_p(i):
                    u, t = u0 + i, todo[i][0]
                    pe.wait_ge(scaled, 4 * (u + 1))
                    if u:
                        pe.wait_ge(pt_act, u)
                    if second_tiles(u - 1) and u:
                        pe.wait_ge(pt_dve, second_tiles(u - 1))
                    for s in range(t + 1):
                        for j in range(4):
                            last = tr(PS[:, 4 + s, j * P:j * P + P], t_S[:, u % 2, j, s * P:s * P + P], ident)
                    last.then_inc(pt_ps, 1)

                def value(i):
                    u, (t, g, b) = u0 + i, todo[i]
                    pe.wait_ge(pt_act, u + 1)
                    if t:
                        pe.wait_ge(pt_dve, second_tiles(u))
                    if i and todo[i - 1][0] != t:
                        if finish:
                            finish(0)
                        pe.wait_ge(z_ready, 2 * zstage[stage] + 1)
                    values(t, g, b, t_PT[:, u % 2, :, :, :]).then_inc(pv_done, 1)

                score(0)
                for i in range(len(todo)):
                    if i + 1 < len(todo):
                        score(i + 1)
                    if i:
                        value(i - 1)
                    turn_p(i)
                value(len(todo) - 1)
                if finish:
                    finish(1)

            def per_head_values(V):
                def values(t, g, b, PT):
                    for j in range(4):
                        for s in range(t + 1):
                            last = mm(O_ps[:, 4 * g + j, :], V(s, 4 * g + j), PT[:, s, j, :],
                                      start=s == 0, stop=s == t, skip_group_check=True)
                    return last
                return values

            pe.wait_ge(con_in, 16)
            pe.wait_ge(params_in, 16 * 10)
            tr(PS[:, 0, 0:P], rowsb[:, :], ident).then_inc(par_ps, 1)

            turn("ffn0")
            ffn(0)

            turn("mlstm")
            for c in range(3):
                chunk("mlstm", c)
            o = side("m_rows")
            pe.wait_ge(chunk_act, first_chunk["mlstm"] + 1)
            pe.wait_ge(chunk_dve, first_chunk["mlstm"] + 1)
            for w in range(2):
                for t in range(NT):
                    last = tr(o[0:HEADS, w * T + t * P:w * T + t * P + P], m_g[:, t, 8 * w:8 * w + 8], ident)
            last.then_inc(side_ps, 1)
            chunk("mlstm", 3)
            for name, row in (("m_a", grow[0]), ("m_floor", grow[1])):
                o = side(name)
                pe.wait_ge(side_src, src_no[name])
                for t in range(NT):
                    last = tr(o[:, 8 * t:8 * t + 8], row[:, t * P:t * P + P], con[0:HEADS, 0:HEADS])
                last.then_inc(side_ps, 1)
            chunk("mlstm", 4)

            def rows_of_heads(name, row, j):
                o = side(name)
                for i in range(2):
                    hh = 2 * j + i
                    last = mm(o[:, i * T:i * T + T], con[0:HEADS, hh:hh + 1].to_broadcast([HEADS, P]), row,
                              start=True, stop=True, skip_group_check=True)
                last.then_inc(side_ps, 1)

            for j in range(2):
                rows_of_heads(f"m_M{j}", grow[3], j)
            chunk("mlstm", 5)
            for j in range(2, 4):
                rows_of_heads(f"m_M{j}", grow[3], j)
            chunk("mlstm", 6)

            def m_scores(hh):
                if hh >= 4:
                    pe.wait_ge(m_w, hh - 3)
                half = slice(64 * (hh % 2), 64 * (hh % 2) + 64)
                mm(PS[:, hh % 4, 0:T], m_kT[half, hh // 2, 0:P], m_qT[half, hh // 2, :],
                   start=True, stop=True, skip_group_check=True)
                mm(PS[:, hh % 4, T:384], m_kT[half, hh // 2, P:T], m_qT[half, hh // 2, P:T],
                   start=True, stop=True, skip_group_check=True).then_inc(m_st, 1)

            def m_numerator(hh):
                pe.wait_ge(m_w, hh + 1)
                if hh >= 4:
                    pe.wait_ge(m_out, hh - 3)
                o = PS[:, 4 + hh % 4, :]
                mm(o[:, 0:129], m_E[:, hh, 0:P], m_v[:, 0, hh, :], start=True, stop=True, skip_group_check=True)
                mm(o[:, T:T + 129], m_E[:, hh, P:T], m_v[:, 0, hh, :], start=True, stop=False, skip_group_check=True)
                mm(o[:, T:T + 129], m_E[:, hh, T:384], m_v[:, 1, hh, :], start=False, stop=True,
                   skip_group_check=True).then_inc(m_num, 1)

            pe.wait_ge(chunk_act, first_chunk["mlstm"] + 7)
            pe.wait_ge(chunk_dve, first_chunk["mlstm"] + 7)
            pe.wait_ge(pads_ready, 2)
            for hh in range(2):
                m_scores(hh)
            for hh in range(HEADS):
                if hh + 2 < HEADS:
                    m_scores(hh + 2)
                m_numerator(hh)
            turn("mlstm_out")
            out_stage("mlstm_out")
            turn("ffn1")
            ffn(1)

            turn("kv")
            chunk("kv", 0)
            chunk("kv", 1)
            pe.wait_ge(chunk_act, first_chunk["kv"] + 1)
            pe.wait_ge(chunk_dve, first_chunk["kv"] + 1)
            for c in range(4):
                if c == 2:
                    chunk("kv", 2)
                o = side(f"ct{c}")
                for i in range(2):
                    for t in range(NT):
                        last = tr(o[:, i * T + t * P:i * T + t * P + P], v_cd[:, t, 2 * c + i, :, :], ident)
                last.then_inc(side_ps, 1)
            for c in range(4):
                b, hp = c // 2, c % 2
                o = side(f"kt{c}")
                pe.wait_ge(side_src, src_no["keys"])
                for i in range(2):
                    for t in range(NT):
                        last = tr(o[:, i * T + t * P:i * T + t * P + P], v_kd[:, b, t, 2 * hp + i, :, :], ident)
                last.then_inc(side_ps, 1)
            for kv in range(2):
                o = side(f"c{kv}")
                pe.wait_ge(side_src, src_no[f"c{kv}"])
                for i in range(2):
                    p = first_piece["cmp"] + 2 * kv + i
                    pe.wait_ge(lo_done, p + 1)
                    wh, wl = parts(p, 8)
                    for k in range(8):
                        l = 8 * i + k
                        last = three(o[:, 0:256], FH[:, l, :, :], FL[:, l, :, :], wh[:, k, :], wl[:, k, :],
                                     start=l == 0, stop=l == 15)
                    last.then_inc(used, 1)
                o = side(f"c{kv}T")
                pe.wait_ge(side_src, src_no[f"c{kv}T"])
                for k in range(2):
                    last = tr(o[:, k * P:k * P + P], v_sc[:, k * P:k * P + P], ident)
                last.then_inc(side_ps, 1)
                pe.wait_ge(side_act, looks(side_no[f"c{kv}T"], "act"))
                if kv == 0:
                    o = side("kcmp")
                    for k in range(2):
                        last = mm(o[:, 0:HD], v_scT[:, k, :], w2s[:, 0, k, :], start=k == 0, stop=k == 1,
                                  skip_group_check=True)
                    last.then_inc(side_ps, 1)
                    o = side("kcmpT")
                    pe.wait_ge(side_src, src_no["kcmpT"])
                    tr(o[:, 0:P], v_kd[:, 0, 0, 0, :, :], ident).then_inc(side_ps, 1)
                else:
                    o = side("vcmp")
                    for g in range(KVH):
                        for k in range(2):
                            last = mm(o[:, g * HD:g * HD + HD],
                                      v_rep[:, k, g, :, :],
                                      w2s[:, 1, k, :], start=k == 0, stop=k == 1, skip_group_check=True)
                    last.then_inc(side_ps, 1)

            turn("ffn2")
            ffn(2)

            turn("nsa")
            for c in range(3):
                chunk("nsa", c)
            pe.wait_ge(q_norm, 1)
            for j in range(4):
                for k in (2 * j, 2 * j + 1):
                    for t in range(NT):
                        last = tr(PS[:, 4 + j, (k % 2) * T + t * P:(k % 2) * T + t * P + P],
                                  xs[:, t, k * P:k * P + P], ident)
                last.then_inc(q_ps, 1)
            pe.wait_ge(qT_act, 2)
            pe.wait_ge(qT_dve, 2)
            for t in range(NT):
                for k in range(KT):
                    last = mm(PS[:, t, 64 * k:64 * k + 64], n_qT[:, k, t * P:t * P + P], KB[:, k // 2, :],
                              start=True, stop=True, skip_group_check=True)
                last.then_inc(cs_ps, 1)

            def turn_cmp():
                pe.wait_ge(cs_neg, 2)
                for t in range(NT):
                    for g in range(KVH):
                        last = tr(PS[:, 4 + t, g * P:g * P + P], n_cs[:, t, 4 * g:4 * g + 4, :], ident)
                    last.then_inc(cs_ps, 1)
                pe.wait_ge(cs_exp, 2)
                pe.wait_ge(cs_neg, 3)

            turn_cmp()

            def n_scores(o, t, g, b, j, w):
                half = slice(64 * (j % 2), 64 * (j % 2) + 64)
                return mm(o, n_qT[half, 2 * g + j // 2, t * P:t * P + P], KTS[half, b, g, 0:w], start=True, stop=True,
                          skip_group_check=True)

            def n_values(t, g, b, PT):
                if b == 0:
                    for jj in range(2):
                        mm(O_ps[:, 2 * g + jj, :], VB[:, g, jj, :], n_cpT[:, t, g, :], start=jj == 0, stop=False,
                           skip_group_check=True)
                for s in range(t + 1):
                    for par_ in range(2):
                        last = mm(O_ps[64 * par_:64 * par_ + 64, 2 * g:2 * g + 2, :],
                                  VTS[:, b, s, HD * g:HD * g + HD], PT[:, s, par_:4:2, :], start=False,
                                  stop=b == 1 and s == t, skip_group_check=True)
                return last

            attend("nsa", n_scores, n_values)
            pe.wait_ge(z_ready, 2)
            out_stage("nsa_out")
            turn("ffn3")
            ffn(3)

            turn("fox")
            for c in range(3):
                chunk("fox", c)
            pe.wait_ge(chunk_act, first_chunk["fox"] + 1)
            pe.wait_ge(chunk_dve, first_chunk["fox"] + 1)
            o = side("f_rows")
            for t in range(NT):
                last = tr(o[0:HEADS, t * P:t * P + P], f_f[:, t, :], ident)
            last.then_inc(side_ps, 1)
            chunk("fox", 3)
            chunk("fox", 4)
            pe.wait_ge(side_src, src_no["f_cum"])
            rows_of_heads("f_C0", grow[3], 0)
            rows_of_heads("f_C1", grow[3], 1)
            chunk("fox", 5)
            rows_of_heads("f_C2", grow[3], 2)
            rows_of_heads("f_C3", grow[3], 3)
            for c in range(6, 9):
                chunk("fox", c)
            pe.wait_ge(chunk_act, first_chunk["fox"] + 9)
            pe.wait_ge(chunk_dve, first_chunk["fox"] + 9)

            def f_scores(o, t, g, b, j, w):
                last = mm(o, f_qT[:, 4 * g + j, t * P:t * P + P], f_kT[:, 4 * g + j, 0:w], start=True, stop=t == 1,
                          skip_group_check=True)
                if t == 0:
                    last = mm(o, ident, caus[:, P:2 * P], start=False, stop=True, skip_group_check=True)
                return last

            attend("fox", f_scores,
                   per_head_values(lambda s, hh: f_v[:, s, hh * P:hh * P + P]))
            pe.wait_ge(z_ready, 4)
            out_stage("fox_out")

            turn("dsa")
            for c in range(4):
                chunk("dsa", c)
                if c == 2:
                    pe.wait_ge(wuk_in, 32)
                    pe.wait_ge(pads_ready, 7)
                    for w in range(2):
                        o = side(f"wuk{w}")
                        for i in range(4):
                            last = tr(o[:, i * P:i * P + P], d_wukr[:, 4 * w + i, :], ident)
                        last.then_inc(side_ps, 1)
            pe.wait_ge(side_src, src_no["qi"])
            for w in range(2):
                o = side(f"qi{w}")
                for i in range(2):
                    for t in range(NT):
                        m = 2 * w + i
                        last = tr(o[:, i * T + t * P:i * T + t * P + P], d_qi[:, t, m * P:m * P + P], ident)
                last.then_inc(side_ps, 1)
            chunk("dsa", 4)
            pe.wait_ge(side_src, src_no["ki_ckv"])
            o = side("ki_ckv")
            for t in range(NT):
                tr(o[:, t * P:t * P + P], d_kid[:, t, :, :], ident)
                last = tr(o[:, T + t * P:T + t * P + P], d_ckr[:, t, 0:P], ident)
            last.then_inc(side_ps, 1)
            o = side("kr")
            for t in range(NT):
                last = tr(o[0:32, t * P:t * P + P], d_ckr[:, t, P:P + 32], ident)
            last.then_inc(side_ps, 1)
            pe.wait_ge(side_act, looks(side_no["ki_ckv"], "act"))
            pe.wait_ge(side_dve, looks(side_no["kr"], "dve"))
            for i in range(6):
                t, heads = index_parts[i]
                o, w = side(f"idx{i}"), P * (t + 1)
                for j, hh in enumerate(heads):
                    half = slice(64 * (hh % 2), 64 * (hh % 2) + 64)
                    last = mm(o[:, j * w:j * w + w], d_qiT[half, hh // 2, t * P:t * P + P], d_kiT[half, 0:w],
                              start=True, stop=True, skip_group_check=True)
                last.then_inc(side_ps, 1)
                if i == 3:
                    chunk("dsa", 5)
            chunk("dsa", 6)
            pe.wait_ge(q_norm, 2)
            pe.wait_ge(chunk_act, first_chunk["dsa"] + 7)
            pe.wait_ge(chunk_dve, first_chunk["dsa"] + 7)
            for j in range(4):
                for k in (2 * j, 2 * j + 1):
                    for t in range(NT):
                        last = tr(PS[:, j, (k % 2) * T + t * P:(k % 2) * T + t * P + P],
                                  xs[:, t, k * P:k * P + P], ident)
                last.then_inc(q_ps, 1)
            pe.wait_ge(qT_act, 4)
            pe.wait_ge(qT_dve, 4)
            for j in range(4):
                o = side(f"ql{j}")
                for i in range(2):
                    last = mm(o[:, i * T:i * T + T], d_wukT[:, 2 * j + i, :], d_qT[:, 2 * j + i, :],
                              start=True, stop=True, skip_group_check=True)
                last.then_inc(side_ps, 1)
            pe.wait_ge(side_act, looks(side_no["ql3"], "act"))
            pe.wait_ge(side_dve, looks(side_no["ql3"], "dve"))

            def d_scores(o, t, g, b, j, w):
                hh = 4 * g + j
                mm(o, d_ql[:, hh, t * P:t * P + P], d_ckvT[:, 0:w], start=True, stop=False, skip_group_check=True)
                return mm(o, d_qT[0:32, hh, t * P:t * P + P], d_krT[0:32, 0:w], start=False, stop=True,
                          skip_group_check=True)

            def uv(t):
                pe.wait_ge(ol_ready, t + 1)
                for hh in range(HEADS):
                    last = mm(O_ps[:, hh, :], d_wuv[:, hh, :], d_ol[:, hh, :], start=True, stop=True,
                              skip_group_check=True)
                last.then_inc(uv_done, 1)

            attend("dsa", d_scores, per_head_values(lambda s, hh: d_ckr[:, s, 0:P]), uv)
            pe.wait_ge(z_ready, 6)
            out_stage("dsa_out")

        @block.scalar
        def _(act):
            A = nc.scalar.activation
            steps = [0]
            split = [0]

            def link(ins):
                steps[0] += 1
                ins.then_inc(act_step, 1)
                act.wait_ge(act_step, steps[0])

            def hi(p, n=PIECE, it=None):
                act.wait_ge(landed[p % RAW], counted(it, 32 * 6 // RAW, 32 * (p // RAW + 1)))
                if p >= SPL:
                    act.wait_ge(used, counted(it, 6, p - SPL + 1))
                A(whi[:, p % SPL, 0:n], raw[:, p % RAW, 0:n], ACT.Copy).then_inc(hi_done, 1)

            def split_to(p_end):
                for p in range(split[0], min(p_end, NP)):
                    hi(p, pieces[p][1] if pieces[p] else PIECE)
                split[0] = max(split[0], min(p_end, NP))

            def rms_norm(name):
                if before[name]:
                    act.wait_ge(h_first, before[name])
                else:
                    act.wait_ge(x_in, 32)
                if name != "ffn0":
                    act.wait_ge(turned, 4 * turns.index(name))
                A(xs[:, 0, :], h[:, 0, :], ACT.Square, accum_out=ss[:, 0:1]).then_inc(ss_act, 1)
                act.wait_ge(root_out, roots.index(name) + 1)
                A(xs[:, 0, :], h[:, 0, :], ACT.Identity, scale=rr[:, 0:1]).then_inc(xs_act, 1)

            def turn(name):
                u = turns.index(name)
                for j in range(4):
                    act.wait_ge(turned, 4 * u + j + 1)
                    if name in gains:
                        for k in (2 * j, 2 * j + 1):
                            last = A(XH[:, k, :], PS[:, 4 + j, (k % 2) * T:(k % 2) * T + T], ACT.Identity,
                                     scale=par[:, gains[name] + k:gains[name] + k + 1])
                    else:
                        last = A(XH[:, 2 * j:2 * j + 2, :].rearrange("p k t -> p (k t)"), PS[:, 4 + j, :], ACT.Copy)
                    last.then_inc(turned_hi, 1)

            def ffn(f):
                p0, n0 = first_piece[f"ffn{f}"], f * NI

                def exps(t, n, it=None):
                    if t == 0:
                        act.wait_ge(a_ready, counted(it, 2, n + 1))
                    A(ffe[:, t, :], PS[:, 4 + t, 0:FC], ACT.Sigmoid).then_inc(exp_done, 1)

                def g_hi(n, it=None):
                    act.wait_ge(g_turned, counted(it, 2, n + 1))
                    A(GH[:, :, :].rearrange("p k t -> p (k t)"), PS[:, 6, :], ACT.Copy).then_inc(gh_done, 1)

                def step(i, it=None):
                    n = n0 + i
                    p = p0 + 2 + 3 * (i - 1)
                    exps_after = (0, 1, None)
                    for j in range(3):
                        hi(p + AHEAD + j, it=it)
                        if exps_after[j] == 1:
                            act.wait_ge(used, counted(it, 6, p + 2))
                        if exps_after[j] is not None:
                            exps(j, n, it)
                    g_hi(n, it)

                split_to(p0 + AHEAD)
                split_to(p0 + AHEAD + 1)
                exps(0, n0)
                split_to(p0 + AHEAD + 2)
                act.wait_ge(used, p0 + 2)
                exps(1, n0)
                g_hi(n0)
                step(1)
                with nc.scalar.Fori(0, (NI - 3) // 2) as it:
                    for j in range(2):
                        step(2 + j, it)
                i = NI - 1
                n, p = n0 + i, p0 + 2 + 3 * (i - 1)
                split[0] = p + AHEAD
                split_to(p + AHEAD + 1)
                exps(0, n)
                split_to(p + AHEAD + 2)
                act.wait_ge(used, p + 2)
                exps(1, n)
                g_hi(n)
                split_to(p + AHEAD + 4)

            def bank_of(stage, c, odd):
                return PS[:, 2 * ((first_chunk[stage] + c) % 3) + odd, :]

            def even_bank(stage, c):
                split_to(chunk_end(stage, c) + AHEAD)
                act.wait_ge(chunk_ps, first_chunk[stage] + c + 1)
                return bank_of(stage, c, 0)

            def side(name):
                act.wait_ge(side_ps, made(side_no[name]))
                return PS[:, 6 + side_no[name] % 2, :]

            def two(x):
                return x.rearrange("p (m t) -> p m t", m=2)

            def attend(stage, finish):
                todo, u0 = units[stage], unit0[stage]

                def exps(i):
                    u, w = u0 + i, P * (todo[i][0] + 1)
                    for j in range(4):
                        c = 4 * u + j
                        act.wait_ge(masked, c + 1)
                        A(t_S[:, u % 2, j, 0:w], t_S[:, u % 2, j, 0:w], ACT.Exp, scale=-1.0, bias=nmin[:, c:c + 1],
                          accum_out=zsum[:, c:c + 1]).then_inc(expd, 1)

                exps(0)
                for i in range(len(todo)):
                    if i + 1 < len(todo):
                        exps(i + 1)
                    act.wait_ge(pt_ps, u0 + i + 1)
                    A(t_PT[:, (u0 + i) % 2, 0, :, :].rearrange("p j t -> p (j t)"), PS[:, 4, :], ACT.Copy)\
                        .then_inc(pt_act, 1)
                    if i and todo[i - 1][0] != todo[i][0]:
                        finish(0, u0 + i)
                finish(1, u0 + len(todo))

            def z_parts(stage):
                def finish(t, _):
                    act.wait_ge(z_raw, 2 * (zstage[stage] - 1) + t + 1)
                    A(XH[:, :, t * P:t * P + P], z_mix, ACT.Copy).then_inc(z_hi, 1)
                return finish

            act.dma_start(h[:, 0, :], a["x"][0, 0:P, :]).then_inc(x_in, 16)
            act.dma_start(con[:, :], a["con"]).then_inc(con_in, 16)
            rms_norm("ffn0")
            act.wait_ge(par_ready, 1)
            turn("ffn0")
            split_to(AHEAD)
            act.wait_ge(small_in, 48)
            ffn(0)

            rms_norm("mlstm")
            turn("mlstm")
            o = even_bank("mlstm", 0)
            A(m_g[:, 0, :], o[:, 0:16], ACT.Copy).then_inc(chunk_act, 1)
            for c in (1, 2):
                o = even_bank("mlstm", c)
                A(m_og[:, 0, 512 * (c - 1):512 * c], o, ACT.Copy).then_inc(chunk_act, 1)
            o = side("m_rows")
            link(A(grow[0], o[0:HEADS, 0:T], ACT.Identity, bias=bif[:, 0:1]))
            A(grow[1], o[0:HEADS, T:2 * T], ACT.Identity, bias=bif[:, 1:2]).then_inc(side_act, 1)

            def log_forget(n):
                act.wait_ge(for_act, for_act_no[f"abs{n}"])
                A(grow[2], grow[2], ACT.Sigmoid, scale=-1.0).then_inc(by_act, 1)

            log_forget(0)
            act.wait_ge(chunk_act, first_chunk["mlstm"] + 3)
            act.wait_ge(chunk_dve, first_chunk["mlstm"] + 3)
            A(m_og, m_og, ACT.Sigmoid).then_inc(by_act, 1)
            o = even_bank("mlstm", 3)
            A(m_v[:, 0, 0:4, 0:P], o.rearrange("p (h d) -> p h d", h=4), ACT.Copy).then_inc(chunk_act, 1)
            o = side("m_floor")
            A(m_floor, o[:, 0:16].rearrange("p (t h) -> p t h", t=NT), ACT.Exp, scale=-1.0).then_inc(side_act, 1)
            o = even_bank("mlstm", 4)
            A(m_v[:, 0, 4:8, 0:P], o.rearrange("p (h d) -> p h d", h=4), ACT.Copy).then_inc(chunk_act, 1)

            def decay(j):
                o = side(f"m_M{j}")
                act.wait_ge(side_dve, looks(side_no["m_a"], "dve"))
                for i in range(2):
                    hh = 2 * j + i
                    A(m_E[:, hh, 0:T], o[:, i * T:i * T + T], ACT.Sigmoid, scale=-1.0, bias=m_a[:, 0, hh:hh + 1])
                    last = A(m_E[:, hh, T:384], o[:, i * T + P:i * T + T], ACT.Sigmoid, scale=-1.0,
                             bias=m_a[:, 1, hh:hh + 1])
                last.then_inc(side_act, 1)

            decay(0)
            decay(1)
            o = even_bank("mlstm", 5)
            A(m_qT[:, 0:2, :], two(o), ACT.Copy).then_inc(chunk_act, 1)
            decay(2)
            decay(3)
            o = even_bank("mlstm", 6)
            A(m_kT[:, 0:2, :], two(o), ACT.Copy).then_inc(chunk_act, 1)
            for hh in range(HEADS):
                for t in range(NT):
                    act.wait_ge(m_out, 2 * hh + t + 1)
                    last = A(m_E[:, hh, t * P:t * P + P], xs[:, t, hh * P:hh * P + P], ACT.Square,
                             accum_out=ss[:, 8 * t + hh:8 * t + hh + 1])
                last.then_inc(head_sq, 1)
            turn("mlstm_out")
            split_to(piece_end("mlstm_out") + AHEAD)
            rms_norm("ffn1")
            turn("ffn1")
            ffn(1)

            rms_norm("kv")
            turn("kv")

            def dup8(x):
                return x.rearrange("p (c d) -> p c d", c=8).unsqueeze(2).to_broadcast([P, 8, 2, HD])

            o = even_bank("kv", 0)
            A(v_cd[:, 0, :, :, :], dup8(o), ACT.Copy).then_inc(chunk_act, 1)

            def kv_halves(c):
                o = even_bank("kv", c)
                A(v_k[:, c - 1, 0, :, :], o[:, 0:256].rearrange("p (h d) -> p h d", h=KVH), ACT.Copy)
                A(VTS[:, c - 1, 0, :], o[:, 256:512], ACT.Copy).then_inc(chunk_act, 1)

            def shifted(name, c):
                o = side(name)
                A(v_ct[0:64, 2 * c:2 * c + 2, :], two(o)[0:64, :, :], ACT.Copy)
                A(v_ct[64:128, 2 * c:2 * c + 2, 0:T - 1], two(o)[64:128, :, 1:T], ACT.Copy).then_inc(side_act, 1)

            kv_halves(1)
            shifted("ct0", 0)
            kv_halves(2)
            shifted("ct2", 2)
            for c in (0, 2):
                o = side(f"kt{c}")
                b = c // 2
                A(KTS[:, b, 0:2, :], two(o), ACT.Identity, scale=par[:, R_KN + 1 + b:R_KN + 2 + b]).then_inc(side_act, 1)
            split_to(first_piece["cmp"] + AHEAD)
            for kv in range(2):
                act.wait_ge(for_act, for_act_no[f"block{kv}"])
                act.wait_ge(pads_ready, 6)
                A(FH[:, :, :, 0:NCMP], v_fs, ACT.Copy).then_inc(by_act, 1)
                split_to(first_piece["cmp"] + 2 * kv + 2 + AHEAD)
                act.wait_ge(used, first_piece["cmp"] + 2 * kv + 2)
                A(v_sc, PS[:, 6 + side_no[f"c{kv}"] % 2, 0:256], ACT.Sigmoid).then_inc(by_act, 1)
                o = side(f"c{kv}T")
                if kv == 0:
                    A(v_scT[:, :, :].rearrange("p k m -> p (k m)"), o[:, 0:256], ACT.Copy).then_inc(side_act, 1)
                else:
                    for k in range(2):
                        src = o[:, k * P:k * P + P].rearrange("p (g n) -> p g n", g=KVH)
                        last = A(v_rep[:, k, :, :, :], src.unsqueeze(2).to_broadcast([P, KVH, 4, 32]), ACT.Copy)
                    last.then_inc(side_act, 1)
            rms_norm("ffn2")
            turn("ffn2")
            ffn(2)

            rms_norm("nsa")
            turn("nsa")
            for c in (0, 1):
                o = even_bank("nsa", c)
                A(xs[:, 0, 512 * c:512 * c + 512], o, ACT.Copy).then_inc(chunk_act, 1)
            o = even_bank("nsa", 2)
            A(n_gt[:, 0, :], o[:, 0:48], ACT.Copy).then_inc(chunk_act, 1)
            act.wait_ge(chunk_act, first_chunk["nsa"] + 3)
            act.wait_ge(chunk_dve, first_chunk["nsa"] + 3)
            A(n_gt, n_gt, ACT.Sigmoid).then_inc(by_act, 1)
            for j in (0, 2):
                act.wait_ge(q_ps, j + 1)
                A(n_qT[:, 2 * j:2 * j + 2, :], two(PS[:, 4 + j, :]), ACT.Identity, scale=qgain[:, 0:1])\
                    .then_inc(qT_act, 1)
            act.wait_ge(cs_neg, 1)
            A(n_cs, n_cs, ACT.Exp, scale=-1.0).then_inc(cs_exp, 1)
            act.wait_ge(cs_ps, 3)
            A(n_cpT[:, 0, :, :].rearrange("p g q -> p (g q)"), PS[:, 4, :], ACT.Copy).then_inc(cs_exp, 1)

            def n_finish(t, u):
                act.wait_ge(pv_done, u)
                A(XH[:, :, t * P:t * P + P], O_ps, ACT.Copy).then_inc(z_hi, 1)

            attend("nsa", n_finish)
            split_to(piece_end("nsa_out") + AHEAD)
            rms_norm("ffn3")
            turn("ffn3")
            ffn(3)

            turn("fox")
            o = even_bank("fox", 0)
            A(f_f[:, 0, :], o[:, 0:8], ACT.Copy).then_inc(chunk_act, 1)

            def silu_sigmoid(stage, c, m):
                o = even_bank(stage, c)
                A(f_gate[:, m:m + 2, :], two(o), ACT.Sigmoid)
                act.wait_ge(used, chunk_end(stage, c))
                A(f_gate[:, m + 2:m + 4, :], two(bank_of(stage, c, 1)), ACT.Sigmoid).then_inc(chunk_act, 1)

            silu_sigmoid("fox", 1, 0)
            silu_sigmoid("fox", 2, 4)
            o = side("f_rows")
            A(grow[1], o[0:HEADS, 0:T], ACT.Identity, bias=bif[:, 2:3]).then_inc(side_act, 1)
            log_forget(1)
            for c in (3, 4):
                o = even_bank("fox", c)
                A(f_v[:, 0, 512 * (c - 3):512 * (c - 3) + 512], o, ACT.Copy).then_inc(chunk_act, 1)
            for c in (5, 6):
                o = even_bank("fox", c)
                A(f_qT[:, 4 * (c - 5):4 * (c - 5) + 2, :], two(o), ACT.Copy, scale=-float(P) ** -0.5)\
                    .then_inc(chunk_act, 1)
            for c in (7, 8):
                o = even_bank("fox", c)
                A(f_kT[:, 4 * (c - 7):4 * (c - 7) + 2, :], two(o), ACT.Copy).then_inc(chunk_act, 1)
            attend("fox", z_parts("fox"))
            split_to(piece_end("fox_out") + AHEAD)

            def layer_norm(name):
                act.wait_ge(for_act, for_act_no[name])
                A(scr[:, :], xs[:, 0, :], ACT.Square, accum_out=ss[:, 0:1]).then_inc(by_act, 1)

            layer_norm("ln0")

            turn("dsa")
            for c, dst in ((0, d_ckr[:, 0, 0:160]), (1, d_kiwi[:, 0, 0:72]), (2, d_qi[:, 0, :])):
                o = even_bank("dsa", c)
                A(dst, o[:, 0:dst.shape[1]], ACT.Copy).then_inc(chunk_act, 1)
            o = side("wuk0")
            A(d_wukT[:, 0:4, :].rearrange("p h c -> p (h c)"), o, ACT.Copy).then_inc(side_act, 1)
            o = even_bank("dsa", 3)
            A(xs[:, 0, 0:512], o, ACT.Copy).then_inc(chunk_act, 1)
            o = side("qi0")
            A(d_qiT[:, 0:2, :], two(o), ACT.Copy).then_inc(side_act, 1)
            o = even_bank("dsa", 4)
            A(xs[:, 0, 512:1024], o, ACT.Copy).then_inc(chunk_act, 1)
            o = side("ki_ckv")
            A(d_kiT, o[:, 0:T], ACT.Copy)
            A(d_ckvT, o[:, T:2 * T], ACT.Identity, scale=par[:, R_CKV:R_CKV + 1]).then_inc(side_act, 1)
            for i in range(6):
                o = side(f"idx{i}")
                if i >= 2:
                    act.wait_ge(idx_acc, i - 1)
                A(S_idx[:, i % 2, :], o, ACT.Relu, scale=0.125).then_inc(side_act, 1)
                if i == 3:
                    silu_sigmoid("dsa", 5, 0)
            silu_sigmoid("dsa", 6, 4)
            for j in (0, 2):
                act.wait_ge(q_ps, 4 + j + 1)
                A(d_qT[:, 2 * j:2 * j + 2, :], two(PS[:, j, :]), ACT.Copy, scale=-float(P) ** -0.5).then_inc(qT_act, 1)
            for j in (0, 2):
                o = side(f"ql{j}")
                A(d_ql[:, 2 * j:2 * j + 2, :], two(o), ACT.Copy).then_inc(side_act, 1)
            dsa_parts = z_parts("dsa")

            def d_finish(t, u):
                act.wait_ge(pv_done, u)
                A(d_ol, O_ps, ACT.Identity, scale=par[:, R_CKV:R_CKV + 1]).then_inc(ol_ready, 1)
                dsa_parts(t, u)

            attend("dsa", d_finish)
            split_to(NP)
            layer_norm("ln1")

        @block.vector
        def _(dve):
            V = nc.vector
            steps = [0]
            split = [0]

            def link(ins):
                steps[0] += 1
                ins.then_inc(dve_step, 1)
                dve.wait_ge(dve_step, steps[0])

            def lo(p, n=PIECE, it=None):
                dve.wait_ge(hi_done, counted(it, 6, p + 1))
                V.tensor_tensor(wlo[:, p % SPL, 0:n], raw[:, p % RAW, 0:n], whi[:, p % SPL, 0:n].bitcast(F32),
                                ALU.subtract).then_inc(lo_done, 1)

            def split_to(p_end):
                for p in range(split[0], min(p_end, NP)):
                    lo(p, pieces[p][1] if pieces[p] else PIECE)
                split[0] = max(split[0], min(p_end, NP))

            def root(name, w):
                y, v, t_ = ry[:, 0:w], rv[:, 0:w], rt[:, 0:w]
                link(V.tensor_scalar(y.bitcast(U32), v.bitcast(U32), 1, None, ALU.logical_shift_right))
                V.tensor_scalar(v, v, -0.5, None, ALU.mult).then_inc(dve_step, 1)
                steps[0] += 1
                link(V.tensor_scalar(y.bitcast(I32), y.bitcast(I32), -1.0, float(0x5F3759DF), ALU.mult, ALU.add))
                for i in range(3):
                    link(V.tensor_tensor(t_, y, y, ALU.mult))
                    link(V.tensor_tensor(t_, t_, v, ALU.mult))
                    if i < 2:
                        link(V.scalar_tensor_tensor(out=y, in0=t_, scalar=1.5, in1=y, op0=ALU.add, op1=ALU.mult))
                V.scalar_tensor_tensor(out=rr[:, 0:w], in0=t_, scalar=1.5, in1=y, op0=ALU.add, op1=ALU.mult)\
                    .then_inc(root_out, 1)
                dve.wait_ge(root_out, roots.index(name) + 1)

            def mean_square(w, n, eps):
                link(V.tensor_scalar(rv[:, 0:w], ss[:, 0:w], 1.0 / n, eps, ALU.mult, ALU.add))

            def rms_norm(name):
                if before[name] == 0:
                    dve.wait_ge(x_in, 32)
                else:
                    dve.wait_ge(turned, 4 * turns.index(name))
                link(V.tensor_tensor_reduce(xs[:, 1, :], h[:, 1, :], h[:, 1, :], 1.0, 0.0, ALU.mult, ALU.add,
                                            ss[:, 1:2]))
                dve.wait_ge(ss_act, rms.index(name) + 1)
                mean_square(2, D, EPS)
                root(name, 2)
                V.tensor_scalar(xs[:, 1, :], h[:, 1, :], rr[:, 1:2], None, ALU.mult).then_inc(xs_dve, 1)

            def turn(name):
                u = turns.index(name)
                for j in range(4):
                    dve.wait_ge(turned_hi, 4 * u + j + 1)
                    if name in gains:
                        for k in (2 * j, 2 * j + 1):
                            last = V.scalar_tensor_tensor(
                                out=XL[:, k, :], in0=PS[:, 4 + j, (k % 2) * T:(k % 2) * T + T],
                                scalar=par[:, gains[name] + k:gains[name] + k + 1], in1=XH[:, k, :].bitcast(F32),
                                op0=ALU.mult, op1=ALU.subtract)
                    else:
                        last = V.tensor_tensor(XL[:, 2 * j:2 * j + 2, :], two(PS[:, 4 + j, :]),
                                               XH[:, 2 * j:2 * j + 2, :].bitcast(F32), ALU.subtract)
                    last.then_inc(x_ready, 1)

            def two(x):
                return x.rearrange("p (m t) -> p m t", m=2)

            def update(name, scale, stage=None):
                dve.wait_ge(acc_first, updates[name])
                for t in range(NT):
                    if t == 1:
                        dve.wait_ge(used, piece_end(name))
                    for w in range(2):
                        part = h[:, t, 512 * w:512 * w + 512]
                        last = V.scalar_tensor_tensor(out=part, in0=acc_ps[:, t, w, :], scalar=scale, in1=part,
                                                      op0=ALU.mult, op1=ALU.add)
                    if t == 0:
                        last.then_inc(h_first, 1)
                last.then_inc(h_ready, 1)
                dve.wait_ge(h_ready, updates[name])

            def ffn(f):
                p0, n0 = first_piece[f"ffn{f}"], f * NI

                def silu(t, n, it=None):
                    e, g, q = ffe[:, t, :], ffg[:, t, :], 2 * n + t
                    dve.wait_ge(exp_done, counted(it, 4, q + 1))
                    if n:
                        dve.wait_ge(g_turned, counted(it, 2, n))
                    V.tensor_tensor(g, e, PS[:, 4 + t, 0:FC], ALU.mult).then_inc(silu_step, 1)
                    dve.wait_ge(silu_step, counted(it, 4, q + 1))
                    V.tensor_tensor(g, g, PS[:, 4 + t, FC:2 * FC], ALU.mult).then_inc(gated, 1)

                def g_lo(n, it=None):
                    dve.wait_ge(gh_done, counted(it, 2, n + 1))
                    V.tensor_tensor(GL[:, :, :], two(PS[:, 6, :]), GH[:, :, :].bitcast(F32), ALU.subtract)\
                        .then_inc(gl_done, 1)

                def step(i, it=None):
                    n, p = n0 + i, p0 + 2 + 3 * (i - 1)
                    lo(p + AHEAD, it=it)
                    silu(0, n, it)
                    lo(p + AHEAD + 1, it=it)
                    silu(1, n, it)
                    lo(p + AHEAD + 2, it=it)
                    g_lo(n, it)

                split_to(p0 + AHEAD + 1)
                silu(0, n0)
                split_to(p0 + AHEAD + 2)
                silu(1, n0)
                g_lo(n0)
                step(1)
                with nc.vector.Fori(0, (NI - 3) // 2) as it:
                    for j in range(2):
                        step(2 + j, it)
                i = NI - 1
                n, p = n0 + i, p0 + 2 + 3 * (i - 1)
                split[0] = p + AHEAD
                split_to(p + AHEAD + 1)
                silu(0, n)
                split_to(p + AHEAD + 2)
                silu(1, n)
                g_lo(n)
                split_to(p + AHEAD + 4)
                update(f"ffn{f}", 0.5)

            def bank_of(stage, c, odd):
                return PS[:, 2 * ((first_chunk[stage] + c) % 3) + odd, :]

            def odd_bank(stage, c):
                split_to(chunk_end(stage, c) + AHEAD)
                dve.wait_ge(used, chunk_end(stage, c))
                return bank_of(stage, c, 1)

            def side(name):
                dve.wait_ge(side_ps, made(side_no[name]))
                return PS[:, 6 + side_no[name] % 2, :]

            def attend(stage, masks, finish, gate=None):
                todo, u0 = units[stage], unit0[stage]

                def mask(i):
                    (t, g, b), u = todo[i], u0 + i
                    w = P * (t + 1)
                    dve.wait_ge(s_ready, u + 1)
                    if u >= 2:
                        dve.wait_ge(pt_ps, u - 1)
                    bank = PS[:, 2 * (u % 2):2 * (u % 2) + 2, :].rearrange("p b n -> p (b n)")
                    for j in range(4):
                        V.tensor_tensor_reduce(t_S[:, u % 2, j, 0:w], bank[:, place(j, w):place(j, w) + w], masks(t, g, j), 1.0, BIG * 4,
                                               ALU.add, ALU.min, nmin[:, 4 * u + j:4 * u + j + 1]).then_inc(masked, 1)

                def scale(i):
                    (t, g, b), u = todo[i], u0 + i
                    w = P * (t + 1)
                    r = rz[:, 4 * u:4 * u + 4]
                    dve.wait_ge(expd, 4 * u + 4)
                    link(V.reciprocal(r, zsum[:, 4 * u:4 * u + 4]))
                    if gate:
                        link(V.tensor_tensor(r, r, gate(t, g, b), ALU.mult))
                    for j in range(4):
                        V.tensor_scalar(t_S[:, u % 2, j, 0:w], t_S[:, u % 2, j, 0:w], rz[:, 4 * u + j:4 * u + j + 1],
                                        None, ALU.mult).then_inc(scaled, 1)

                mask(0)
                for i in range(len(todo)):
                    if i + 1 < len(todo):
                        mask(i + 1)
                    scale(i)
                    if todo[i][0]:
                        dve.wait_ge(pt_ps, u0 + i + 1)
                        V.tensor_copy(t_PT[:, (u0 + i) % 2, 1, :, :].rearrange("p j t -> p (j t)"), PS[:, 5, :])\
                            .then_inc(pt_dve, 1)
                    if i and todo[i - 1][0] != todo[i][0]:
                        finish(0, u0 + i)
                finish(1, u0 + len(todo))

            def low_of_z(stage, t, z):
                dve.wait_ge(z_hi, 2 * zstage[stage] + t + 1)
                V.tensor_tensor(XL[:, :, t * P:t * P + P], z, XH[:, :, t * P:t * P + P].bitcast(F32), ALU.subtract)\
                    .then_inc(z_ready, 1)

            def layer_norm(name, i):
                dve.wait_ge(acc_first, updates[f"ln{i}"])
                for t in range(NT):
                    if t == 1:
                        dve.wait_ge(used, piece_end(f"{name}_out"))
                    for w in range(2):
                        part = h[:, t, 512 * w:512 * w + 512]
                        last = V.scalar_tensor_tensor(out=part, in0=part, scalar=ALPHA, in1=acc_ps[:, t, w, :],
                                                      op0=ALU.mult, op1=ALU.add,
                                                      accum_out=lns[:, 2 * t + w:2 * t + w + 1])
                link(last)
                link(V.tensor_tensor(lns[:, 4:6], lns[:, 0:4:2], lns[:, 1:4:2], ALU.add))
                link(V.tensor_scalar(lns[:, 6:8], lns[:, 4:6], -1.0 / D, None, ALU.mult))
                V.tensor_scalar(xs[:, 0, :], h[:, 0, :], lns[:, 6:7], None, ALU.add).then_inc(for_act, 1)
                link(V.tensor_scalar(xs[:, 1, :], h[:, 1, :], lns[:, 7:8], None, ALU.add))
                link(V.tensor_tensor_reduce(h[:, 1, :], xs[:, 1, :], xs[:, 1, :], 1.0, 0.0, ALU.mult, ALU.add,
                                            ss[:, 1:2]))
                dve.wait_ge(by_act, by_act_no[f"ln{i}"])
                mean_square(2, D, LN_EPS)
                root(f"ln{i}", 2)
                dve.wait_ge(ln_in, 32 * (i + 1))
                for t in range(NT):
                    last = V.scalar_tensor_tensor(out=xs[:, t, :], in0=xs[:, t, :], scalar=rr[:, t:t + 1],
                                                  in1=LNB[:, 0, :], op0=ALU.mult, op1=ALU.mult)
                link(last)
                V.tensor_tensor(h[:, 0, :], xs[:, 0, :], LNB[:, 1, :], ALU.add).then_inc(first_tile, 1)
                V.tensor_tensor(h[:, 1, :], xs[:, 1, :], LNB[:, 1, :], ALU.add).then_inc(h_ready, 1)
                dve.wait_ge(h_ready, updates[f"ln{i}"])

            rms_norm("ffn0")
            dve.wait_ge(par_ps, 1)
            V.tensor_copy(par[:, :], PS[:, 0, 0:P]).then_inc(par_ready, 1)
            dve.wait_ge(par_ready, 1)
            link(V.tensor_scalar(qgain[:, :], par[:, R_QN:R_QN + 1], -float(HD) ** -0.5, None, ALU.mult))
            turn("ffn0")
            split_to(AHEAD)
            ffn(0)

            rms_norm("mlstm")
            turn("mlstm")
            o = odd_bank("mlstm", 0)
            V.tensor_copy(m_g[:, 1, :], o[:, 0:16]).then_inc(chunk_dve, 1)
            for c in (1, 2):
                o = odd_bank("mlstm", c)
                V.tensor_copy(m_og[:, 1, 512 * (c - 1):512 * c], o).then_inc(chunk_dve, 1)

            def log_forget(n, rows_name):
                u, e, sq, q = grow[1], grow[2], grow[3], xs[0:HEADS, 0, 0:T]
                dve.wait_ge(side_act, looks(side_no[rows_name], "act"))
                V.scalar_tensor_tensor(out=e, in0=u, scalar=-1.0, in1=u, op0=ALU.mult, op1=ALU.max).then_inc(for_act, 1)
                link(V.tensor_scalar(u, u, 0.0, None, ALU.min))
                dve.wait_ge(by_act, by_act_no[f"log{n}"])
                link(V.tensor_scalar(q, e, -1.0, 2.0, ALU.mult, ALU.add))
                link(V.reciprocal(q, q))
                link(V.tensor_tensor(e, e, q, ALU.mult))
                link(V.tensor_tensor(sq, e, e, ALU.mult))
                link(V.tensor_scalar(q, sq, 1.0 / 13, None, ALU.mult))
                for k in (11, 9, 7, 5, 3):
                    link(V.scalar_tensor_tensor(out=q, in0=q, scalar=1.0 / k, in1=sq, op0=ALU.add, op1=ALU.mult))
                link(V.scalar_tensor_tensor(out=q, in0=q, scalar=1.0, in1=e, op0=ALU.add, op1=ALU.mult))
                link(V.scalar_tensor_tensor(out=u, in0=q, scalar=-2.0, in1=u, op0=ALU.mult, op1=ALU.add))
                V.tensor_tensor_scan(e, u, zcol[0:HEADS, :].to_broadcast([HEADS, T]), 0.0, ALU.add, ALU.add)\
                    .then_inc(dve_step, 1)
                steps[0] += 1
                dve.wait_ge(dve_step, steps[0])

            log_forget(0, "m_rows")
            V.tensor_tensor(grow[0], grow[0], grow[2], ALU.subtract).then_inc(side_src, 1)
            dve.wait_ge(side_src, 1)
            link(V.tensor_tensor_scan(grow[3], zcol[0:HEADS, :].to_broadcast([HEADS, T]), grow[0], 0.0,
                                      ALU.add, ALU.max))
            V.tensor_tensor(grow[1], grow[2], grow[3], ALU.add).then_inc(side_src, 1)
            o = odd_bank("mlstm", 3)
            V.tensor_copy(m_v[:, 1, 0:4, 0:P], o.rearrange("p (h d) -> p h d", h=4)).then_inc(chunk_dve, 1)
            o = side("m_a")
            V.tensor_copy(m_a, o[:, 0:16].rearrange("p (t h) -> p t h", t=NT)).then_inc(side_dve, 1)
            o = odd_bank("mlstm", 4)
            V.tensor_copy(m_v[:, 1, 4:8, 0:P], o.rearrange("p (h d) -> p h d", h=4)).then_inc(chunk_dve, 1)

            def decay(j):
                dve.wait_ge(side_act, looks(side_no[f"m_M{j}"], "act"))
                sg = m_E[:, 2 * j:2 * j + 2, :]
                rest = xs[:, j % 2, 0:768].rearrange("p (h t) -> p h t", h=2)
                link(V.tensor_scalar(rest, sg, 0.75, -1.0, ALU.min, ALU.add))
                link(V.reciprocal(rest, rest))
                V.scalar_tensor_tensor(out=sg, in0=sg, scalar=-1.0, in1=rest, op0=ALU.mult, op1=ALU.mult).then_inc(m_decay, 1)
                dve.wait_ge(m_decay, j + 1)

            decay(0)
            decay(1)
            o = odd_bank("mlstm", 5)
            V.tensor_copy(m_qT[:, 2:4, :], two(o)).then_inc(chunk_dve, 1)
            decay(2)
            o = odd_bank("mlstm", 6)
            V.tensor_copy(m_kT[:, 2:4, :], two(o)).then_inc(chunk_dve, 1)
            decay(3)

            def m_weights(hh):
                dve.wait_ge(m_diag, 2 * (hh // 2 + 1))
                dve.wait_ge(m_st, hh + 1)
                V.scalar_tensor_tensor(out=m_E[:, hh, :], in0=PS[:, hh % 4, 0:384], scalar=0.125, in1=m_E[:, hh, :],
                                       op0=ALU.mult, op1=ALU.mult).then_inc(m_w, 1)

            m_weights(0)
            m_weights(1)
            for hh in range(HEADS):
                if hh + 2 < HEADS:
                    m_weights(hh + 2)
                dve.wait_ge(m_num, hh + 1)
                o = PS[:, 4 + hh % 4, :]
                rd = m_tok[:, 32 + 2 * hh:34 + 2 * hh]
                den = o.rearrange("p (t n) -> p t n", t=NT)[:, :, 128:129].rearrange("p t n -> p (t n)")
                link(V.scalar_tensor_tensor(out=rd, in0=den, scalar=-1.0, in1=m_floor[:, :, hh],
                                            op0=ALU.mult, op1=ALU.max))
                link(V.tensor_tensor(rd, rd, den, ALU.max))
                link(V.reciprocal(rd, rd))
                for t in range(NT):
                    V.tensor_scalar(xs[:, t, hh * P:hh * P + P], o[:, t * T:t * T + P], rd[:, t:t + 1], None,
                                    ALU.mult).then_inc(m_out, 1)
            dve.wait_ge(by_act, by_act_no["og"])
            dve.wait_ge(head_sq, HEADS)
            mean_square(16, P, EPS)
            root("head", 16)
            for t in range(NT):
                for hh in range(HEADS):
                    cols = slice(hh * P, hh * P + P)
                    c = 8 * t + hh
                    last = V.scalar_tensor_tensor(out=xs[:, t, cols], in0=xs[:, t, cols], scalar=rr[:, c:c + 1],
                                                  in1=m_og[:, t, cols], op0=ALU.mult, op1=ALU.mult)
            last.then_inc(xs_dve, 1)
            turn("mlstm_out")
            split_to(piece_end("mlstm_out") + AHEAD)
            update("mlstm_out", 1.0)
            rms_norm("ffn1")
            turn("ffn1")
            ffn(1)

            rms_norm("kv")
            turn("kv")

            def dup8(x):
                return x.rearrange("p (c d) -> p c d", c=8).unsqueeze(2).to_broadcast([P, 8, 2, HD])

            o = odd_bank("kv", 0)
            V.tensor_copy(v_cd[:, 1, :, :, :], dup8(o)).then_inc(chunk_dve, 1)

            def kv_halves(c):
                o = odd_bank("kv", c)
                V.tensor_copy(v_k[:, c - 1, 1, :, :], o[:, 0:256].rearrange("p (h d) -> p h d", h=KVH))
                V.tensor_copy(VTS[:, c - 1, 1, :], o[:, 256:512]).then_inc(chunk_dve, 1)

            def shifted(name, c):
                o = side(name)
                V.tensor_copy(v_ct[0:64, 2 * c:2 * c + 2, :], two(o)[0:64, :, :])
                V.tensor_copy(v_ct[64:128, 2 * c:2 * c + 2, 0:T - 1], two(o)[64:128, :, 1:T]).then_inc(side_dve, 1)

            kv_halves(1)
            shifted("ct1", 1)
            kv_halves(2)
            shifted("ct3", 3)
            dve.wait_ge(chunk_dve, first_chunk["kv"] + 3)
            dve.wait_ge(chunk_act, first_chunk["kv"] + 3)
            k16 = v_k.rearrange("p b t h d -> p (b t h) d")
            kd16 = v_kd.rearrange("p b t h u d -> p (b t h) u d")
            sq16 = v_kd.rearrange("p b t h u d -> p (b t h u d)")[:, 0:1024].rearrange("p (c d) -> p c d", c=16)
            link(V.tensor_tensor(sq16, k16, k16, ALU.mult))
            link(V.tensor_reduce(ss[:, 0:16], sq16, AX, ALU.add))
            mean_square(16, HD, EPS)
            root("keys", 16)
            V.tensor_tensor(kd16, k16.unsqueeze(2).to_broadcast([P, 16, 2, HD]),
                            rr[:, 0:16].unsqueeze(2).unsqueeze(3).to_broadcast([P, 16, 2, HD]), ALU.mult)\
                .then_inc(side_src, 1)
            for c in (1, 3):
                o = side(f"kt{c}")
                b = c // 2
                V.tensor_scalar(KTS[:, b, 2:4, :], two(o), par[:, R_KN + 1 + b:R_KN + 2 + b], None, ALU.mult)\
                    .then_inc(side_dve, 1)
            split_to(first_piece["cmp"] + AHEAD)
            dve.wait_ge(turned, 4 * (turns.index("kv") + 1))
            for kv in range(2):
                dve.wait_ge(side_act, looks(side_no["ct2"], "act"))
                dve.wait_ge(side_dve, looks(side_no["ct3"], "dve"))
                if kv:
                    dve.wait_ge(used, first_piece["cmp"] + 2)
                for g in range(KVH):
                    src = v_ct[:, 4 * kv + g, 0:T].rearrange("p (n s) -> p s n", s=16)
                    for half in range(2):
                        last = V.tensor_tensor(
                            v_fs[:, 8 * half:8 * half + 8, g, :],
                            src[:, 0:16:2, half:half + NCMP],
                            par[:, R_PE + 16 * kv + 8 * half:R_PE + 16 * kv + 8 * half + 8].unsqueeze(2)
                            .to_broadcast([P, 8, NCMP]), ALU.add)
                last.then_inc(for_act, 1)
                dve.wait_ge(for_act, for_act_no[f"block{kv}"])
                dve.wait_ge(by_act, by_act_no[f"fh{kv}"])
                V.tensor_tensor(FL[:, :, :, 0:NCMP], v_fs, FH[:, :, :, 0:NCMP].bitcast(F32), ALU.subtract)\
                    .then_inc(side_src, 1)
                split_to(first_piece["cmp"] + 2 * kv + 2 + AHEAD)
                dve.wait_ge(by_act, by_act_no[f"c{kv}"])
                V.tensor_tensor(v_sc, v_sc, PS[:, 6 + side_no[f"c{kv}"] % 2, 0:256], ALU.mult).then_inc(side_src, 1)
                dve.wait_ge(side_src, src_no[f"c{kv}T"])
                if kv == 0:
                    o = side("kcmp")
                    kc = v_kd[:, 0, 0, 0, :, :]
                    kc2 = v_kd[:, 0, 0, 1, 0, :]
                    V.tensor_copy(kc2, o[:, 0:HD]).then_inc(side_dve, 1)
                    dve.wait_ge(side_dve, looks(side_no["kcmp"], "dve"))
                    link(V.tensor_tensor_reduce(kc[:, 0, :], kc2, kc2, 1.0, 0.0, ALU.mult, ALU.add, ss[:, 0:1]))
                    mean_square(1, HD, EPS)
                    root("kcmp", 1)
                    V.tensor_scalar(kc, kc2.unsqueeze(1).to_broadcast([P, 2, HD]), rr[:, 0:1], None, ALU.mult)\
                        .then_inc(side_src, 1)
                    o = side("kcmpT")
                    for half in range(2):
                        q = slice(64 * half, 64 * half + 64)
                        last = V.tensor_scalar(KB[q, :, 32 * half:32 * half + 32],
                                               o[q, 0:P].rearrange("p (h n) -> p h n", h=KVH), par[q, R_KN:R_KN + 1],
                                               None, ALU.mult)
                    last.then_inc(side_dve, 1)
                else:
                    o = side("vcmp")
                    for j in range(4):
                        q = slice(32 * j, 32 * j + 32)
                        last = V.tensor_copy(VB[q, :, j // 2, HD * (j % 2):HD * (j % 2) + HD],
                                             o[q, 0:256].rearrange("p (h d) -> p h d", h=KVH))
                    last.then_inc(side_dve, 1)
            rms_norm("ffn2")
            turn("ffn2")
            ffn(2)

            rms_norm("nsa")
            turn("nsa")
            for c in (0, 1):
                o = odd_bank("nsa", c)
                V.tensor_copy(xs[:, 1, 512 * c:512 * c + 512], o).then_inc(chunk_dve, 1)
            dve.wait_ge(chunk_act, first_chunk["nsa"] + 2)
            dve.wait_ge(chunk_dve, first_chunk["nsa"] + 2)
            xs32 = xs[:, :, :].rearrange("p t (h d) -> p (t h) d", d=HD)
            sq32 = wide.rearrange("p (h d) -> p h d", d=HD)
            link(V.tensor_tensor(sq32, xs32, xs32, ALU.mult))
            link(V.tensor_reduce(ss[:, 0:32], sq32, AX, ALU.add))
            o = odd_bank("nsa", 2)
            V.tensor_copy(n_gt[:, 1, :], o[:, 0:48]).then_inc(chunk_dve, 1)
            mean_square(32, HD, EPS)
            root("q", 32)
            V.tensor_tensor(xs32, xs32, rr[:, 0:32].unsqueeze(2).to_broadcast([P, 32, HD]), ALU.mult)\
                .then_inc(q_norm, 1)
            dve.wait_ge(by_act, by_act_no["gates"])
            for j in (1, 3):
                dve.wait_ge(q_ps, j + 1)
                V.tensor_scalar(n_qT[:, 2 * j:2 * j + 2, :], two(PS[:, 4 + j, :]), qgain[:, 0:1], None, ALU.mult)\
                    .then_inc(qT_dve, 1)
            cm_min, cm_sum = n_cm[:, 0:32], n_cm[:, 32:64]
            cs32 = n_cs.rearrange("p t h n -> p (t h) n")
            dve.wait_ge(cs_ps, 2)
            for t in range(NT):
                last = V.tensor_tensor(n_cs[:, t, :, :], PS[:, t, :].rearrange("p (h n) -> p h n", h=QH),
                                       cmask[:, t:t + 1, :].to_broadcast([P, QH, 32]), ALU.add)
            link(last)
            link(V.tensor_reduce(cm_min, cs32, AX, ALU.min))
            V.tensor_tensor(cs32, cs32, cm_min.unsqueeze(2).to_broadcast([P, 32, 32]), ALU.subtract)\
                .then_inc(cs_neg, 1)
            dve.wait_ge(cs_exp, 1)
            for t in range(NT):
                last = V.tensor_tensor(n_cs[:, t, :, :], n_cs[:, t, :, :],
                                       ckeep[:, t:t + 1, :].to_broadcast([P, QH, 32]), ALU.mult)
            link(last)
            link(V.tensor_reduce(cm_sum, cs32, AX, ALU.add))
            link(V.tensor_scalar(cm_sum, cm_sum, 1e-30, None, ALU.max))
            link(V.reciprocal(cm_sum, cm_sum))
            link(V.tensor_tensor(cm_sum.rearrange("p (t h) -> p t h", t=NT), cm_sum.rearrange("p (t h) -> p t h", t=NT),
                                 n_gt[:, :, 0:QH], ALU.mult))
            V.tensor_tensor(cs32, cs32, cm_sum.unsqueeze(2).to_broadcast([P, 32, 32]), ALU.mult).then_inc(cs_neg, 1)
            dve.wait_ge(cs_ps, 4)
            V.tensor_copy(n_cpT[:, 1, :, :].rearrange("p g q -> p (g q)"), PS[:, 5, :]).then_inc(cs_neg, 1)

            def n_finish(t, u):
                low_of_z("nsa", t, O_ps)

            attend("nsa", lambda t, g, j: caus[:, P * (1 - t):2 * P], n_finish,
                   lambda t, g, b: n_gt[:, t, QH * (b + 1) + 4 * g:QH * (b + 1) + 4 * g + 4])
            split_to(piece_end("nsa_out") + AHEAD)
            update("nsa_out", 1.0)
            rms_norm("ffn3")
            turn("ffn3")
            ffn(3)

            V.tensor_copy(lns[:, 0:1], h[:, 0, 0:1]).then_inc(xs_dve, 1)
            turn("fox")
            o = odd_bank("fox", 0)
            V.tensor_copy(f_f[:, 1, :], o[:, 0:8]).then_inc(chunk_dve, 1)

            def silu_gate(stage, c, m):
                split_to(chunk_end(stage, c) + AHEAD)
                dve.wait_ge(chunk_act, first_chunk[stage] + c + 1)
                g = f_gate[:, m:m + 4, :]
                b0 = 2 * ((first_chunk[stage] + c) % 3)
                V.tensor_tensor(g, g, PS[:, b0:b0 + 2, :].rearrange("p b (m t) -> p (b m) t", m=2), ALU.mult)\
                    .then_inc(chunk_dve, 1)

            silu_gate("fox", 1, 0)
            silu_gate("fox", 2, 4)
            log_forget(1, "f_rows")
            V.tensor_copy(grow[3], grow[2]).then_inc(side_src, 1)
            for c in (3, 4):
                o = odd_bank("fox", c)
                V.tensor_copy(f_v[:, 1, 512 * (c - 3):512 * (c - 3) + 512], o).then_inc(chunk_dve, 1)

            def gate_sums(j):
                o = two(side(f"f_C{j}"))
                V.tensor_tensor(f_cm[:, 2 * j:2 * j + 2, :], o, caus.unsqueeze(1).to_broadcast([P, 2, T]), ALU.add)\
                    .then_inc(side_dve, 1)

            gate_sums(0)
            gate_sums(1)
            for c in (5, 6):
                o = odd_bank("fox", c)
                V.tensor_scalar(f_qT[:, 4 * (c - 5) + 2:4 * (c - 5) + 4, :], two(o), -float(P) ** -0.5, None, ALU.mult)\
                    .then_inc(chunk_dve, 1)
                if c == 5:
                    gate_sums(2)
                    gate_sums(3)
            for c in (7, 8):
                o = odd_bank("fox", c)
                V.tensor_copy(f_kT[:, 4 * (c - 7) + 2:4 * (c - 7) + 4, :], two(o)).then_inc(chunk_dve, 1)

            def gated_z(stage, t):
                V.tensor_tensor(z_mix, O_ps, f_gate[:, :, t * P:t * P + P], ALU.mult).then_inc(z_raw, 1)
                low_of_z(stage, t, z_mix)

            def f_finish(t, u):
                dve.wait_ge(pv_done, u)
                gated_z("fox", t)

            attend("fox", lambda t, g, j: f_cm[:, 4 * g + j, 0:P * (t + 1)], f_finish)
            split_to(piece_end("fox_out") + AHEAD)
            layer_norm("fox", 0)

            V.tensor_copy(lns[:, 0:1], h[:, 0, 0:1]).then_inc(xs_dve, 1)
            turn("dsa")
            for c, dst in ((0, d_ckr[:, 1, 0:160]), (1, d_kiwi[:, 1, 0:72]), (2, d_qi[:, 1, :])):
                o = odd_bank("dsa", c)
                V.tensor_copy(dst, o[:, 0:dst.shape[1]]).then_inc(chunk_dve, 1)
            o = side("wuk1")
            V.tensor_copy(d_wukT[:, 4:8, :].rearrange("p h c -> p (h c)"), o).then_inc(side_dve, 1)
            dve.wait_ge(chunk_act, first_chunk["dsa"] + 3)
            dve.wait_ge(chunk_dve, first_chunk["dsa"] + 3)

            def rope(x, n, half, table):
                tab = con[:, table:table + 4 * half].rearrange("p (w t f) -> p w t f", w=2, t=NT)
                for t in range(NT):
                    x1, x2 = x[:, t, :, 0:half], x[:, t, :, half:2 * half]
                    c = tab[:, 0, t:t + 1, :].to_broadcast([P, n, half])
                    s = tab[:, 1, t:t + 1, :].to_broadcast([P, n, half])
                    m = n * half
                    a1, a2 = (d_ra[:, i * P:i * P + m].rearrange("p (n f) -> p n f", n=n) for i in range(2))
                    b1, b2 = (d_rb[:, i * P:i * P + m].rearrange("p (n f) -> p n f", n=n) for i in range(2))
                    V.tensor_tensor(a1, x1, c, ALU.mult)
                    V.tensor_tensor(a2, x2, s, ALU.mult)
                    V.tensor_tensor(b1, x2, c, ALU.mult)
                    link(V.tensor_tensor(b2, x1, s, ALU.mult))
                    V.tensor_tensor(x1, a1, a2, ALU.subtract)
                    last = V.tensor_tensor(x2, b1, b2, ALU.add)
                    if t < NT - 1:
                        link(last)
                return last

            rope(d_qi.rearrange("p t (h d) -> p t h d", h=8), 8, 8, C_ROPE_I).then_inc(side_src, 1)
            dve.wait_ge(side_src, src_no["qi"])
            for t in range(NT):
                last = V.tensor_tensor_reduce(d_ra[:, 0:P] if t == 0 else d_rb[:, 0:P], d_ckr[:, t, 0:P],
                                              d_ckr[:, t, 0:P], 1.0, 0.0, ALU.mult, ALU.add, ss[:, t:t + 1])
            link(last)
            mean_square(2, P, EPS)
            root("ckv", 2)
            for t in range(NT):
                last = V.tensor_scalar(d_ckr[:, t, 0:P], d_ckr[:, t, 0:P], rr[:, t:t + 1], None, ALU.mult)
            link(last)
            link(rope(d_ckr[:, :, P:P + 32].unsqueeze(2), 1, 16, C_ROPE_A))
            link(rope(d_kiwi[:, :, 0:64].unsqueeze(2), 1, 8, C_ROPE_I))
            V.tensor_scalar(d_w8, d_kiwi[:, :, 64:72], 8.0 ** -0.5, None, ALU.mult)
            V.tensor_copy(d_kid, d_kiwi[:, :, 0:64].unsqueeze(2).to_broadcast([P, NT, 2, 64])).then_inc(side_src, 1)
            dve.wait_ge(side_src, src_no["ki_ckv"])
            o = odd_bank("dsa", 3)
            V.tensor_copy(xs[:, 1, 0:512], o).then_inc(chunk_dve, 1)
            o = side("qi1")
            V.tensor_copy(d_qiT[:, 2:4, :], two(o)).then_inc(side_dve, 1)
            o = odd_bank("dsa", 4)
            V.tensor_copy(xs[:, 1, 512:1024], o).then_inc(chunk_dve, 1)
            o = side("kr")
            V.tensor_copy(d_krT[0:32, :], o[0:32, 0:T]).then_inc(side_dve, 1)

            def index_scores(i):
                t, heads = index_parts[i]
                w = P * (t + 1)
                isc = d_isc[:, 0:P] if t == 0 else d_isc[:, P:384]
                dve.wait_ge(side_act, looks(side_no[f"idx{i}"], "act"))
                for j, hh in enumerate(heads):
                    src, wt = S_idx[:, i % 2, j * w:j * w + w], d_w8[:, t, hh:hh + 1]
                    if hh == 0:
                        last = V.tensor_scalar(isc, src, wt, None, ALU.mult)
                    else:
                        last = V.scalar_tensor_tensor(out=isc, in0=src, scalar=wt, in1=isc, op0=ALU.mult, op1=ALU.add)
                    if j < len(heads) - 1:
                        link(last)
                last.then_inc(idx_acc, 1)
                dve.wait_ge(idx_acc, i + 1)

            def choose(t):
                w = P * (t + 1)
                cols = slice(0, P) if t == 0 else slice(P, 384)
                work, isc, sel_ = d_work[:, cols], d_isc[:, cols], d_sel[:, cols]
                cm = caus[:, P:2 * P] if t == 0 else caus
                link(V.tensor_tensor(work, isc, cm, ALU.subtract))
                for _ in range(8):
                    link(V.max(d_m8, work))
                    link(V.match_replace(work, d_m8, work, -3e38))
                link(V.tensor_scalar(sel_, work, -2e38, BIG, ALU.is_gt, ALU.mult))
                link(V.tensor_tensor(sel_, sel_, cm, ALU.add))

            for i in range(2):
                index_scores(i)
            choose(0)
            for i in range(2, 4):
                index_scores(i)
            silu_gate("dsa", 5, 0)
            for i in range(4, 6):
                index_scores(i)
            dve.wait_ge(chunk_act, first_chunk["dsa"] + 5)
            dve.wait_ge(chunk_dve, first_chunk["dsa"] + 5)
            rope(xs[:, :, :].rearrange("p t (h d) -> p t h d", h=8), 8, 16, C_ROPE_A).then_inc(q_norm, 1)
            choose(1)
            silu_gate("dsa", 6, 4)
            for j in (1, 3):
                dve.wait_ge(q_ps, 4 + j + 1)
                V.tensor_scalar(d_qT[:, 2 * j:2 * j + 2, :], two(PS[:, j, :]), -float(P) ** -0.5, None, ALU.mult)\
                    .then_inc(qT_dve, 1)
            for j in (1, 3):
                o = side(f"ql{j}")
                V.tensor_copy(d_ql[:, 2 * j:2 * j + 2, :], two(o)).then_inc(side_dve, 1)

            def d_finish(t, u):
                dve.wait_ge(uv_done, t + 1)
                gated_z("dsa", t)

            attend("dsa", lambda t, g, j: d_sel[:, 0:P] if t == 0 else d_sel[:, P:384], d_finish)
            split_to(NP)
            layer_norm("dsa", 1)


_INS = ["x", "ffn_norm", "ffn_w_in", "ffn_w_out", "mix_norm", "a_w_in", "a_b_if", "a_g_head", "a_w_out", "kv_norm",
        "kv_w", "cmp_pe", "cmp_w1", "cmp_w2", "k_norm", "b_w_in", "b_q_norm", "b_w_out", "ln_g_2", "ln_b_2",
        "fox_w_in_2", "fox_b_f_2", "fox_w_out_2", "dsa_w_in_2", "dsa_kv_norm_g_2", "dsa_w_uk_2", "dsa_w_uv_2",
        "dsa_w_out_2"]


def kernel(**inputs):
    import concourse.bacc as bacc
    from concourse.bass_utils import run_bass_kernel_spmd

    nc = bacc.Bacc("TRN2", target_bir_lowering=False, num_devices=1)
    arrays, args = {}, {}
    for name in _INS:
        arr = np.ascontiguousarray(inputs[name])
        arrays[f"in_{name}_dram"] = arr
        args[name] = nc.dram_tensor(f"in_{name}_dram", arr.shape, mybir.dt.from_np(arr.dtype),
                                    kind="ExternalInput").ap()
    arr = constant_tables()
    arrays["con_dram"] = arr
    args["con"] = nc.dram_tensor("con_dram", arr.shape, F32, kind="ExternalInput").ap()
    out = nc.dram_tensor("out_0_dram", (1, T, D), F32, kind="ExternalOutput").ap()
    program(nc, args, out)
    r = run_bass_kernel_spmd(nc, [arrays], core_ids=[0])
    return r.results[0]["out_0_dram"]
```
